# Optimizing a Trainium2 kernel written in Bass

```python
import jax, jax.numpy as jnp
from jax import lax
import numpy as np

D_MODEL = 1024
BATCH = 1
SEQ = 256
DEPTH = 2
DEC_BATCH = 8
DEC_SEQ = 4
PAST_LEN = 256
PAGE_SIZE = 128

HEAD_DIM = 64
N_HEADS_A = 8
N_KV_A = 2
N_IDX_HEADS = 4
D_IDX = 64
IDX_TOPK_MAX = 256
N_HEADS_B = 8
N_KV_B = 2
MOBA_BLOCK = 256
MOBA_TOPK_MAX = 3
N_GROUPS = 4
EXPERTS_PER_GROUP = 8
N_EXPERTS = N_GROUPS * EXPERTS_PER_GROUP
D_EXPERT = 256
TOPK_IN_GROUP = 2
MOE_ROW_BLOCK = 128
ROPE_THETA = 10000.0
RMS_EPS = 1e-6
Q_BLOCK_DSA = 128
Q_BLOCK_MOBA = 32

WIDTH_A = N_HEADS_A * HEAD_DIM
KV_WIDTH_A = N_KV_A * HEAD_DIM
WIDTH_B = N_HEADS_B * HEAD_DIM
KV_WIDTH_B = N_KV_B * HEAD_DIM
IN_SPLITS = (WIDTH_A, KV_WIDTH_A, KV_WIDTH_A, N_IDX_HEADS * D_IDX, D_IDX, N_IDX_HEADS,
             WIDTH_B, KV_WIDTH_B, KV_WIDTH_B, D_MODEL, D_MODEL)
D_IN = sum(IN_SPLITS)

kernel_name = 'dsa_moba_hier_moe_decoder_step'

def rms_norm(x, g):
    xf = x.astype(jnp.float32)
    y = xf * lax.rsqrt(jnp.mean(xf * xf, axis=-1, keepdims=True) + RMS_EPS)
    return (y * g.astype(jnp.float32)).astype(x.dtype)

def rope(x, pos):
    half = x.shape[-1] // 2
    inv = jnp.power(ROPE_THETA, -jnp.arange(half, dtype=jnp.float32) / half)
    ang = pos.astype(jnp.float32)[:, None] * inv[None, :]
    cos = jnp.cos(ang)[None, :, None, :]
    sin = jnp.sin(ang)[None, :, None, :]
    xf = x.astype(jnp.float32)
    x1, x2 = xf[..., :half], xf[..., half:]
    return jnp.concatenate([x1 * cos - x2 * sin, x2 * cos + x1 * sin], axis=-1).astype(x.dtype)

def sweep_queries(fn, qargs, block):
    tq = qargs[0].shape[1]
    if tq <= block or tq % block != 0:
        return fn(*qargs)
    nb = tq // block

    def split(a):
        return jnp.moveaxis(a.reshape((a.shape[0], nb, block) + a.shape[2:]), 1, 0)

    out = lax.map(lambda args: fn(*args), tuple(split(a) for a in qargs))
    out = jnp.moveaxis(out, 0, 1)
    return out.reshape((out.shape[0], tq) + out.shape[3:])

def dsa_attention(q, q_idx, w_idx, q_pos, k, v, k_idx, n_keep):
    b, tq, h, dh = q.shape
    kvh = k.shape[2]
    k_pos = jnp.arange(k.shape[1], dtype=jnp.int32)
    logits = jnp.einsum('bthd,bsd->bths', q_idx, k_idx, preferred_element_type=jnp.float32)
    score = jnp.einsum('bths,bth->bts', jax.nn.relu(logits), w_idx.astype(jnp.float32))
    causal = k_pos[None, None, :] <= q_pos[:, :, None]
    score = jnp.where(causal, score, -jnp.inf)
    _, sel = lax.top_k(score, n_keep)
    valid = sel <= q_pos[:, :, None]
    gather = jax.vmap(lambda a, i: a[i])
    k_sel = gather(k, sel)
    v_sel = gather(v, sel)
    qg = q.reshape(b, tq, kvh, h // kvh, dh)
    s = jnp.einsum('btkgd,btskd->btkgs', qg, k_sel, preferred_element_type=jnp.float32) * (dh ** -0.5)
    s = jnp.where(valid[:, :, None, None, :], s, -jnp.inf)
    p = jax.nn.softmax(s, axis=-1)
    o = jnp.einsum('btkgs,btskd->btkgd', p, v_sel, preferred_element_type=jnp.float32)
    return o.reshape(b, tq, h * dh).astype(q.dtype)

def moba_blocks(k, v):
    b, l, kvh, dh = k.shape
    nb = -(-l // MOBA_BLOCK)
    pad = nb * MOBA_BLOCK - l

    def blk(a):
        a = jnp.pad(a, ((0, 0), (0, pad), (0, 0), (0, 0)))
        return a.reshape(b, nb, MOBA_BLOCK, kvh, dh).transpose(0, 3, 1, 2, 4)

    kb, vb = blk(k), blk(v)
    k_means = jnp.mean(kb.astype(jnp.float32), axis=3)
    return kb, vb, k_means

def moba_attention(q, q_pos, k_blocks, v_blocks, k_means, n_sel):
    b, tq, h, dh = q.shape
    kvh, nb = k_blocks.shape[1], k_blocks.shape[2]
    qg = q.reshape(b, tq, kvh, h // kvh, dh)
    own = q_pos // MOBA_BLOCK
    gate = jnp.einsum('btkgd,bknd->btkgn', qg.astype(jnp.float32), k_means)
    past = jnp.arange(nb)[None, None, None, None, :] < own[:, :, None, None, None]
    gate = jnp.where(past, gate, -jnp.inf)
    _, sel = lax.top_k(gate, n_sel)
    sel_valid = sel < own[:, :, None, None, None]
    b_ix = jnp.arange(b)[:, None, None, None]
    kv_ix = jnp.arange(kvh)[None, None, :, None]
    scale = dh ** -0.5
    scores, vals = [], []
    for j in range(n_sel):
        kj = k_blocks[b_ix, kv_ix, sel[..., j]]
        vj = v_blocks[b_ix, kv_ix, sel[..., j]]
        sj = jnp.einsum('btkgd,btkgsd->btkgs', qg, kj, preferred_element_type=jnp.float32) * scale
        scores.append(jnp.where(sel_valid[..., j:j + 1], sj, -jnp.inf))
        vals.append(vj)
    take_own = jax.vmap(lambda a, o: a[:, o])
    k_own = take_own(k_blocks, own)
    v_own = take_own(v_blocks, own)
    s_own = jnp.einsum('btkgd,bktsd->btkgs', qg, k_own, preferred_element_type=jnp.float32) * scale
    own_pos = own[:, :, None] * MOBA_BLOCK + jnp.arange(MOBA_BLOCK, dtype=jnp.int32)[None, None, :]
    own_ok = own_pos <= q_pos[:, :, None]
    s_own = jnp.where(own_ok[:, :, None, None, :], s_own, -jnp.inf)
    p = jax.nn.softmax(jnp.concatenate(scores + [s_own], axis=-1), axis=-1)
    o = jnp.einsum('btkgs,bktsd->btkgd', p[..., n_sel * MOBA_BLOCK:], v_own,
                   preferred_element_type=jnp.float32)
    for j in range(n_sel):
        o = o + jnp.einsum('btkgs,btkgsd->btkgd', p[..., j * MOBA_BLOCK:(j + 1) * MOBA_BLOCK], vals[j],
                           preferred_element_type=jnp.float32)
    return o.reshape(b, tq, h * dh).astype(q.dtype)

def mixer_block(h, pos, past, w_in_l, w_pa_l, w_pb_l, w_out_l):
    b, t, _ = h.shape
    proj = h @ w_in_l
    offsets = np.cumsum(IN_SPLITS)[:-1].tolist()
    qa, ka, va, qi, ki, wi, qb, kb, vb, ga, gb = jnp.split(proj, offsets, axis=-1)
    qa = rope(qa.reshape(b, t, N_HEADS_A, HEAD_DIM), pos)
    ka = rope(ka.reshape(b, t, N_KV_A, HEAD_DIM), pos)
    va = va.reshape(b, t, N_KV_A, HEAD_DIM)
    qi = rope(qi.reshape(b, t, N_IDX_HEADS, D_IDX), pos)
    ki = rope(ki.reshape(b, t, 1, D_IDX), pos)[:, :, 0]
    qb = rope(qb.reshape(b, t, N_HEADS_B, HEAD_DIM), pos)
    kb = rope(kb.reshape(b, t, N_KV_B, HEAD_DIM), pos)
    vb = vb.reshape(b, t, N_KV_B, HEAD_DIM)
    new_rows = (ka, va, ki, kb, vb)
    if past is None:
        ka_all, va_all, ki_all, kb_all, vb_all = new_rows
    else:
        ka_all, va_all, ki_all, kb_all, vb_all = [jnp.concatenate([p_, n_], axis=1)
                                                  for p_, n_ in zip(past, new_rows)]
    n_keys = ka_all.shape[1]
    q_pos = jnp.broadcast_to(pos[None, :], (b, t))
    n_keep = min(IDX_TOPK_MAX, n_keys // 4)
    ya = sweep_queries(lambda q_, qi_, wi_, qp_: dsa_attention(q_, qi_, wi_, qp_, ka_all, va_all, ki_all, n_keep),
                       (qa, qi, wi, q_pos), Q_BLOCK_DSA)
    k_blocks, v_blocks, k_means = moba_blocks(kb_all, vb_all)
    n_sel = min(MOBA_TOPK_MAX, k_blocks.shape[2])
    yb = sweep_queries(lambda q_, qp_: moba_attention(q_, qp_, k_blocks, v_blocks, k_means, n_sel),
                       (qb, q_pos), Q_BLOCK_MOBA)
    merged = jax.nn.sigmoid(ga) * (ya @ w_pa_l) + jax.nn.sigmoid(gb) * (yb @ w_pb_l)
    return merged @ w_out_l, new_rows

def routed_experts(xf, expert_ids, combine, w_eg, w_eu, w_ed):
    n, d = xf.shape
    k = expert_ids.shape[1]
    m = n * k
    flat_e = expert_ids.reshape(m)
    order = jnp.argsort(flat_e)
    sorted_e = flat_e[order]
    counts = jnp.bincount(flat_e, length=N_EXPERTS)
    padded = (counts + MOE_ROW_BLOCK - 1) // MOE_ROW_BLOCK * MOE_ROW_BLOCK
    pad_end = jnp.cumsum(padded)
    pad_start = pad_end - padded
    start = jnp.cumsum(counts) - counts
    dest = pad_start[sorted_e] + jnp.arange(m, dtype=jnp.int32) - start[sorted_e]
    n_blocks = -(-m // MOE_ROW_BLOCK) + N_EXPERTS
    rows = jnp.zeros((n_blocks * MOE_ROW_BLOCK, d), xf.dtype).at[dest].set(xf[order // k])
    block_start = jnp.arange(n_blocks, dtype=jnp.int32) * MOE_ROW_BLOCK
    block_e = jnp.minimum(jnp.searchsorted(pad_end, block_start, side='right'), N_EXPERTS - 1)

    def expert_block(args):
        xb, e = args
        hdn = jax.nn.silu(xb @ w_eg[e]) * (xb @ w_eu[e])
        return hdn @ w_ed[e]

    out = lax.map(expert_block, (rows.reshape(n_blocks, MOE_ROW_BLOCK, d), block_e))
    y_sorted = out.reshape(n_blocks * MOE_ROW_BLOCK, d)[dest]
    y_slots = jnp.zeros((m, d), y_sorted.dtype).at[order].set(y_sorted).reshape(n, k, d)
    return jnp.einsum('nkd,nk->nd', y_slots, combine.astype(y_slots.dtype))

def hier_moe(h, w_rg, b_rg, w_re, b_re, w_eg, w_eu, w_ed):
    b, t, d = h.shape
    hf = h.reshape(b * t, d)
    p_grp = jax.nn.softmax((hf @ w_rg).astype(jnp.float32) + b_rg.astype(jnp.float32), axis=-1)
    g_star = jnp.argmax(p_grp, axis=-1).astype(jnp.int32)
    p_g = jnp.take_along_axis(p_grp, g_star[:, None], axis=-1)
    e_logits = ((hf @ w_re).astype(jnp.float32) + b_re.astype(jnp.float32)).reshape(
        b * t, N_GROUPS, EXPERTS_PER_GROUP)
    in_grp = jnp.take_along_axis(e_logits, g_star[:, None, None], axis=1)[:, 0]
    top_l, top_i = lax.top_k(in_grp, TOPK_IN_GROUP)
    combine = p_g * jax.nn.softmax(top_l, axis=-1)
    expert_ids = g_star[:, None] * EXPERTS_PER_GROUP + top_i.astype(jnp.int32)
    return routed_experts(hf, expert_ids, combine, w_eg, w_eu, w_ed).reshape(b, t, d)

def trunk_layer(x, c, pos, past, w_ada_l, b_ada_l, g_mix_l, w_in_l, w_pa_l, w_pb_l, w_out_l, g_ffn_l,
                w_rg_l, b_rg_l, w_re_l, b_re_l, w_eg_l, w_eu_l, w_ed_l):
    mod = jax.nn.silu(c) @ w_ada_l + b_ada_l
    sh1, sc1, gt1, sh2, sc2, gt2 = [m_[:, None, :] for m_ in jnp.split(mod, 6, axis=-1)]
    h = rms_norm(x, g_mix_l) * (1.0 + sc1) + sh1
    mix, new_rows = mixer_block(h, pos, past, w_in_l, w_pa_l, w_pb_l, w_out_l)
    x = x + gt1 * mix
    h = rms_norm(x, g_ffn_l) * (1.0 + sc2) + sh2
    x = x + gt2 * hier_moe(h, w_rg_l, b_rg_l, w_re_l, b_re_l, w_eg_l, w_eu_l, w_ed_l)
    return x, new_rows

def gather_pages(pool, page_table):
    g = pool[page_table]
    return g.reshape((g.shape[0], g.shape[1] * g.shape[2]) + g.shape[3:])

def setup_inputs(seed: int = 0) -> dict:
    key = jax.random.key(seed)
    ks = jax.random.split(key, 32)
    f32 = jnp.float32
    n_pages = PAST_LEN // PAGE_SIZE
    n_used = DEC_BATCH * n_pages
    n_pool = n_used + n_used // 4

    def nrm(k_, shape, scale=1.0):
        return jax.random.normal(k_, shape, f32) * scale

    page_table = jax.random.permutation(ks[9], n_pool)[:n_used].reshape(DEC_BATCH, n_pages).astype(jnp.int32)
    return {
        'x_prompt': nrm(ks[0], (BATCH, SEQ, D_MODEL)),
        'x_sample': nrm(ks[1], (DEC_BATCH, DEC_SEQ, D_MODEL)),
        'c_prompt': nrm(ks[2], (BATCH, D_MODEL)),
        'c_sample': nrm(ks[3], (DEC_BATCH, D_MODEL)),
        'cache_k_a': nrm(ks[4], (DEPTH, n_pool, PAGE_SIZE, N_KV_A, HEAD_DIM)),
        'cache_v_a': nrm(ks[5], (DEPTH, n_pool, PAGE_SIZE, N_KV_A, HEAD_DIM)),
        'cache_idx_k': nrm(ks[6], (DEPTH, n_pool, PAGE_SIZE, D_IDX)),
        'cache_k_b': nrm(ks[7], (DEPTH, n_pool, PAGE_SIZE, N_KV_B, HEAD_DIM)),
        'cache_v_b': nrm(ks[8], (DEPTH, n_pool, PAGE_SIZE, N_KV_B, HEAD_DIM)),
        'page_table': page_table,
        'w_ada': nrm(ks[10], (DEPTH, D_MODEL, 6 * D_MODEL), 0.5 * D_MODEL ** -0.5),
        'b_ada': nrm(ks[11], (DEPTH, 6 * D_MODEL), 0.01),
        'g_mix': 1.0 + nrm(ks[12], (DEPTH, D_MODEL), 0.01),
        'w_in': nrm(ks[13], (DEPTH, D_MODEL, D_IN), D_MODEL ** -0.5),
        'w_proj_a': nrm(ks[14], (DEPTH, WIDTH_A, D_MODEL), WIDTH_A ** -0.5),
        'w_proj_b': nrm(ks[15], (DEPTH, WIDTH_B, D_MODEL), WIDTH_B ** -0.5),
        'w_out': nrm(ks[16], (DEPTH, D_MODEL, D_MODEL), D_MODEL ** -0.5),
        'g_ffn': 1.0 + nrm(ks[17], (DEPTH, D_MODEL), 0.01),
        'w_router_group': nrm(ks[18], (DEPTH, D_MODEL, N_GROUPS), D_MODEL ** -0.5),
        'b_router_group': nrm(ks[19], (DEPTH, N_GROUPS), 0.01),
        'w_router_expert': nrm(ks[20], (DEPTH, D_MODEL, N_EXPERTS), D_MODEL ** -0.5),
        'b_router_expert': nrm(ks[21], (DEPTH, N_EXPERTS), 0.01),
        'w_exp_gate': nrm(ks[22], (DEPTH, N_EXPERTS, D_MODEL, D_EXPERT), D_MODEL ** -0.5),
        'w_exp_up': nrm(ks[23], (DEPTH, N_EXPERTS, D_MODEL, D_EXPERT), D_MODEL ** -0.5),
        'w_exp_down': nrm(ks[24], (DEPTH, N_EXPERTS, D_EXPERT, D_MODEL), D_EXPERT ** -0.5),
        'g_final': 1.0 + nrm(ks[25], (D_MODEL,), 0.01),
    }

def stack_rows(rows, i):
    return jnp.stack([r[i] for r in rows], axis=0)

def reference(x_prompt, x_sample, c_prompt, c_sample, cache_k_a, cache_v_a, cache_idx_k, cache_k_b, cache_v_b,
              page_table, w_ada, b_ada, g_mix, w_in, w_proj_a, w_proj_b, w_out, g_ffn, w_router_group,
              b_router_group, w_router_expert, b_router_expert, w_exp_gate, w_exp_up, w_exp_down, g_final):
    past_len = page_table.shape[1] * cache_k_a.shape[2]
    pos_p = jnp.arange(x_prompt.shape[1], dtype=jnp.int32)
    pos_s = past_len + jnp.arange(x_sample.shape[1], dtype=jnp.int32)
    xp, xs = x_prompt, x_sample
    rows_p, rows_s = [], []
    for l in range(DEPTH):
        lw = (w_ada[l], b_ada[l], g_mix[l], w_in[l], w_proj_a[l], w_proj_b[l], w_out[l], g_ffn[l],
              w_router_group[l], b_router_group[l], w_router_expert[l], b_router_expert[l],
              w_exp_gate[l], w_exp_up[l], w_exp_down[l])
        xp, rp = trunk_layer(xp, c_prompt, pos_p, None, *lw)
        past = (gather_pages(cache_k_a[l], page_table), gather_pages(cache_v_a[l], page_table),
                gather_pages(cache_idx_k[l], page_table), gather_pages(cache_k_b[l], page_table),
                gather_pages(cache_v_b[l], page_table))
        xs, rs = trunk_layer(xs, c_sample, pos_s, past, *lw)
        rows_p.append(rp)
        rows_s.append(rs)
    y_prompt = rms_norm(xp, g_final)
    y_sample = rms_norm(xs, g_final)
    return (y_prompt, y_sample,
            stack_rows(rows_p, 0), stack_rows(rows_p, 1), stack_rows(rows_p, 3), stack_rows(rows_p, 4),
            stack_rows(rows_p, 2),
            stack_rows(rows_s, 0), stack_rows(rows_s, 1), stack_rows(rows_s, 3), stack_rows(rows_s, 4),
            stack_rows(rows_s, 2))


_drawn_inputs = setup_inputs


def setup_inputs(seed=0):
    import zlib

    import numpy as np

    out = dict(_drawn_inputs(seed))
    spreads = {}
    factors = {'b_ada': 3.634,
     'g_mix': 5.062,
     'g_ffn': 5.35,
     'b_router_group': 4.183,
     'b_router_expert': 6.959,
     'g_final': 5.552}
    for name, (base, spread) in spreads.items():
        noise = np.random.default_rng([zlib.crc32(name.encode()), seed]).standard_normal(out[name].shape)
        drawn = base * np.exp(spread * noise) if base else spread * noise
        out[name] = __import__('jax').numpy.asarray(drawn.astype(out[name].dtype))
    for name, factor in factors.items():
        out[name] = (out[name] * factor).astype(out[name].dtype)
    return out
```

```python
from contextlib import ExitStack

import concourse.bass as bass
import numpy as np
from concourse import mybir

F32 = mybir.dt.float32
I32 = mybir.dt.int32
ALU = mybir.AluOpType
ACT = mybir.ActivationFunctionType
AX = mybir.AxisListType.X

D = 1024
DEPTH = 2
NP, NB, TS = 256, 8, 4
NS = NB * TS
T = NP + NS
PAGE, PAGES, POOL = 128, 2, 20
PAST = PAGE * PAGES
HD = 64
NH, NKV, GQ = 8, 2, 4
NIDX = 4
N_EXP, D_EXP, N_GRP = 32, 256, 4
KEEP_P, KEEP_S = 64, 65
EPS = 1e-6
SCALE = HD ** -0.5
OFF = -1.0e30

KD = D // 128
NCOND = 1 + NB
NMOD = 6 * KD
SH1, SC1, GT1, SH2, SC2, GT2 = (i * KD for i in range(6))

PAIR = 2048
RING = 12
PAIRS = 144
ROUNDS = PAIRS // RING
P_ADA, P_IN = 0, 24
P_QI, P_KW, P_KAB, P_V, P_QA, P_QB, P_GATE = 24, 25, 26, 27, 28, 30, 32
P_PROJ, P_OUT, P_EXP = 40, 44, 48

TB = T // 3
SLOTS = 2 * T
BLK = 32
MAXBLK = T // BLK
SLOTP = SLOTS + BLK
SB = [(i * 128, min(128, SLOTS - i * 128)) for i in range((SLOTS + 127) // 128)]

C_ID, C_ROT, C_ONE, C_LOW, C_SUM, C_ROW = (i * 128 for i in range(6))
C_HEAD = 768
C_COS = C_HEAD + 4
C_SIN = C_COS + T
C_CB0 = C_SIN + T
C_CB1 = C_CB0 + 128
C_SM = C_CB1 + 256
C_REV = C_SM + T
C_END = C_REV + T

S_WR = 0
S_GM = S_WR + KD * 36
S_GF = S_GM + KD
S_BA = S_GF + KD
S_BR = S_BA + NMOD
S_END = S_BR + 36

CHUNKS = ["qi0", "qi1", "ki", "ka", "kb"] + [f"qa{i}" for i in range(4)] + [f"qb{i}" for i in range(4)]
UNITS = [("b", 0, 0), ("b", 0, 1), ("b", 1, 0), ("b", 1, 1), ("b", 2, 0),
         ("a", 0, 0), ("a", 0, 1), ("a", 1, 0), ("a", 1, 1), ("a", 2, 0)]


def turned(u):
    return 1 if UNITS[u][1] == 0 else 2


def plan():
    jobs = ["mod0", "mt0", "mod1", "mt1", "mod2", "mt2", "ss1", "p.qi0", "p.qi1", "r.qi0", "p.ki", "r.qi1", "wi", "r.ki", "p.ka", "p.kb", "r.ka",
            "wrow", "L0.0", "L0.1", "L1.0", "L1.1", "Ls", "r.kb", "v0", "v1", "v2", "score"]
    late = CHUNKS[5:]
    for i, c in enumerate(late):
        jobs += [f"p.{c}"] + ([f"r.{late[i - 1]}"] if i else [])
    jobs += ["r.qb3"]
    gate = 0
    for i in range(len(UNITS) + 1):
        if i < len(UNITS):
            jobs += [f"s{i}.0", f"s{i}.1"]
        if gate < 16:
            jobs += [f"g{gate}"]
            gate += 1
        if i:
            jobs += [f"t{i - 1}.{n}" for n in range(turned(i - 1))]
        if gate < 16:
            jobs += [f"g{gate}"]
            gate += 1
        if i:
            jobs += [f"o{i - 1}"]
    for m in range(KD):
        jobs += [f"ya{m}", f"yb{m}"]
    jobs += [f"out{m}" for m in range(KD)]
    jobs += ["ss2", "router"] + [f"h{n}" for n in range(6)] + ["rank"]
    jobs += [f"x{k}.{h}" for k in range(KD) for h in range(2)]
    jobs += [f"c{s}" for s in range(len(SB))]
    jobs += [f"y{s}.{h}" for s in range(len(SB)) for h in range(2)]
    jobs += [f"z{m}" for m in range(KD)]
    return jobs


PLAN = plan()
NBANK = 4


SOFT = [5 if u[1] == 2 else 7 for u in UNITS]
EXPS = [2 if u[1] == 2 else 4 for u in UNITS]
IX = 68
R_HOT, R_GAP, R_SEL, ROUTE = 21, 22, 35, 58


def soft_end(u):
    return sum(SOFT[:u + 1])


class Banks:

    def __init__(self, full, drained, psum):
        self.full, self.drained, self.psum = full, drained, psum
        self.place = {name: (i % NBANK, i // NBANK) for i, name in enumerate(PLAN)}
        self.per = [len(range(b, len(PLAN), NBANK)) for b in range(NBANK)]

    def ap(self, name):
        return self.psum[self.place[name][0]][:, :]

    def wait_free(self, eng, l, name):
        b, i = self.place[name]
        eng.wait_ge(self.drained[b], l * self.per[b] + (i + 1))

    def wait_full(self, eng, l, name):
        b, i = self.place[name]
        eng.wait_ge(self.full[b], l * self.per[b] + (i + 1))

    def wait_drained(self, eng, l, name):
        b, i = self.place[name]
        eng.wait_ge(self.drained[b], l * self.per[b] + (i + 2))

    def filled(self, ins, name):
        ins.then_inc(self.full[self.place[name][0]], 1)

    def done(self, ins, name):
        ins.then_inc(self.drained[self.place[name][0]], 1)


class Signal:

    def __init__(self, sem, per, ahead=0):
        self.sem, self.per, self.ahead, self.n = sem, per, ahead, 0

    def up(self, ins):
        self.n += 1
        assert self.n <= self.per, (self.sem.name, self.n)
        ins.then_inc(self.sem, 1)

    def wait(self, eng, l, n=None):
        eng.wait_ge(self.sem, l * self.per + ((self.per if n is None else n) + self.ahead))

    def wait_so_far(self, eng, l):
        self.wait(eng, l, self.n)


def bc(ap, shape):
    return ap.to_broadcast(shape)


def decoder_trunk(nc, wstream, small, consts, pages, page_table, x_in, c_in, gfin,
                  y_out, ka_out, kb_out, ki_out, vp_out, vs_out):
    with ExitStack() as ctx:
        def sb(name, shape, dt=F32):
            return ctx.enter_context(nc.sbuf_tensor(name, shape, dt))

        def sem(name):
            return ctx.enter_context(nc.semaphore(name))

        ring = sb("ring", [128, RING, PAIR])
        x = sb("x", [128, KD, T])
        h = sb("h", [128, KD, T])
        mod = sb("mod", [128, NMOD, NCOND])
        gsc = sb("gsc", [128, 2, KD, NCOND])
        sc = sb("sc", [128, KD, 32])
        sm = sb("sm", [128, S_END])
        cs = sb("cs", [128, C_END])
        gf = sb("gf", [128, KD])
        rms = sb("rms", [128, T])
        ka = sb("ka", [128, T])
        kb = sb("kb", [128, T])
        ki = sb("ki", [128, T])
        v = sb("v", [128, 3, 256])
        wi = sb("wi", [128, 3, 4])
        wrow = sb("wrow", [128, 8])
        qpad_i = sb("qpad_i", [128, NB, 32])
        qpad = sb("qpad", [128, NB, 32])
        stat = sb("stat", [128, 4, GQ])
        top = sb("top", [128, 8])
        table = sb("table", [1, 2, N_EXP], I32)
        ptab = sb("ptab", [1, NB * PAGES], I32)
        dest = sb("dest", [128, 12, 3])
        cnt = sb("cnt", [128, 4, N_EXP])
        yb = sb("yb", [128, 256])
        work = sb("work", [128, 19392])

        def carve(at, *shape):
            n = int(np.prod(shape))
            a = work[:, at:at + n]
            if len(shape) == 2:
                return a.rearrange("p (a b) -> p a b", b=shape[1])
            if len(shape) == 3:
                return a.rearrange("p (a b c) -> p a b c", b=shape[1], c=shape[2])
            return a

        q = {c: carve(i * T, T) for i, c in enumerate(["qi0", "qi1"] + CHUNKS[5:])}
        q.update(ki=ki[:, :], ka=ka[:, :], kb=kb[:, :])
        gate = carve(2880, 16, T)
        yT = carve(7488, 8, T)
        pg = carve(9792, NB, 3, PAST)
        scores = [carve(15936 + i * 1024, 1024) for i in range(2)]
        probsT = carve(17984, 2, 512)
        probsN = carve(19008, 256)
        bias_a = [carve(19264, 128), carve(0, 256), carve(256, T)]
        idx = [carve(7488, 128), carve(7616, 256), carve(7872, T)]
        picked = carve(8160, T)
        ropecos = [carve(8448 + i * T, T) for i in range(2)]
        xsq = carve(5120, KD, T)
        xsort = carve(0, KD, SLOTP)
        ysort = carve(5120, KD, SLOTP)
        yrow = carve(0, len(SB), D)
        hrow = carve(10240, 3, D)
        xs = carve(10240, KD, BLK)
        sg = carve(10496, 2, BLK)
        hdn = carve(10560, 2, BLK)
        gu = carve(10624, 512)
        gusum = carve(11136, 4, BLK)
        mraw = [carve(15936 + i * 512, 512) for i in range(2)]
        sel = carve(13312, 3, SLOTS)
        selw = carve(15040, 3, SLOTS)
        comb = carve(16768, len(SB), T)
        iota = carve(18208, SLOTS)
        YHI = 5120 + 4 * SLOTP
        rt = [carve(YHI + i * 128, 128) for i in range(10)]
        eq1 = carve(YHI + 1280, SLOTS)

        P = [ctx.enter_context(nc.psum_tensor(f"ps{i}", [128, 512], F32)) for i in range(8)]
        pgu, pgut, py, pyt = P[4:]
        banks = Banks([sem(f"full{b}") for b in range(NBANK)], [sem(f"drained{b}") for b in range(NBANK)], P[:NBANK])

        w_in = [sem(f"w_in{s}") for s in range(RING)]
        w_free = sem("w_free")
        start_in = sem("start_in")
        small_in = sem("small_in")
        pages1_in = sem("pages1_in")
        pages2_in = sem("pages2_in")
        rows_out = sem("rows_out")
        y_stored = sem("y_stored")
        zeroed = sem("zeroed")
        silu_c = sem("silu_c")
        x_staged = sem("x_staged")
        gu_done, gu_kept, gut_done = sem("gu_done"), sem("gu_kept"), sem("gut_done")
        summed, silu_done, hdn_ready = sem("summed"), sem("silu_done"), sem("hdn_ready")
        y_done, y_kept = sem("y_done"), sem("y_kept")
        yt_done, yt_kept = sem("yt_done"), sem("yt_kept")
        final = sem("final")
        final_ss, final_rt = sem("final_ss"), sem("final_rt")

        mods = Signal(sem("mods"), 2)
        sq = Signal(sem("sq"), 2)
        root = Signal(sem("root"), 2)
        norm = Signal(sem("norm"), 2 * 8)
        normed = Signal(sem("normed"), 2 * 4)
        cosed = Signal(sem("cosed"), len(CHUNKS), 1)
        roped = Signal(sem("roped"), len(CHUNKS), 1)
        padded = Signal(sem("padded"), 12)
        ix = Signal(sem("ix"), IX)
        soft = Signal(sem("soft"), sum(SOFT))
        exps = Signal(sem("exps"), sum(EXPS))
        merged = Signal(sem("merged"), 8)
        xmix = Signal(sem("xmix"), 8)
        route = Signal(sem("route"), ROUTE)
        rexp = Signal(sem("rexp"), 2)
        iotas = Signal(sem("iotas"), 2)
        xmoe = Signal(sem("xmoe"), 8, 1)
        xtmp = Signal(sem("xtmp"), 2 * 8)

        block = ctx.enter_context(nc.Block())

        def within(at):
            return nc.s_assert_within(at, 0, SLOTS, skip_runtime_bounds_check_because="blocks start inside the expert's slots")

        ident = cs[:, C_ID:C_ID + 128]
        ones = cs[:, C_ONE:C_ONE + 128]
        cos, sin = cs[:, C_COS:C_COS + T], cs[:, C_SIN:C_SIN + T]
        cbias = [cs[:, C_CB0:C_CB0 + 128], cs[:, C_CB1:C_CB1 + 256], cs[:, C_SM:C_SM + T]]

        def hold(eng, count):
            eng.reg_alu(count, count, 0, ALU.max)

        def diag(t, rows0, rows, at=0, width=16):
            base = t[rows0:rows0 + rows, 0, at:at + 1]
            return bass.AP(base.tensor, base.offset, [list(base.ap[0]), [64, NB // 2], [48, 2], [1, width]])

        def unit_keys(u):
            return [128, 256, T][UNITS[u][1]]

        def by_seq(ap, n):
            return ap.rearrange("p k (b t) -> p k b t", t=TS)

        @block.sync
        def _(sp):
            def load(i, s):
                sp.dma_start(ring[:, s, :], wstream[i]).then_inc(w_in[s], 16)

            for s in range(RING):
                load(s, s)
            with sp.Fori(1, DEPTH * ROUNDS) as r:
                for s in range(RING):
                    sp.wait_ge(w_free, (r - 1) * RING + (s + 1))
                    load(r * RING + s, s)

        @block.gpsimd
        def _(g):
            nc.gpsimd.memset(qpad_i[:, :, :], 0.0).then_inc(zeroed, 1)
            nc.gpsimd.memset(qpad[:, :, :], 0.0).then_inc(zeroed, 1)
            nc.gpsimd.memset(yb[:, :], 0.0).then_inc(zeroed, 1)
            g.sem_inc(cosed.sem, 1)
            g.wait_ge(zeroed, 3)

            def step(signal, ins):
                signal.up(ins)
                signal.wait_so_far(g, l)
                hold(g, seen)

            g.wait_ge(start_in, 16 * 5)
            seen = g.alloc_register("pool_blocks")
            g.reg_mov(seen, 0)
            with g.Fori(0, DEPTH) as l:
                g.wait_ge(xmoe.sem, l * xmoe.per + 1)
                g.dma_start(sm[:, :], small[l]).then_inc(small_in, 16)

                def load_pages(w0, n, s):
                    for b in range(NB):
                        for p in range(PAGES):
                            page = g.value_load(ptab[0:1, b * PAGES + p:b * PAGES + p + 1], min_val=0, max_val=POOL - 1)
                            src = pages[bass.ds(page + l * POOL, 1), :, w0 * 128:(w0 + n) * 128]
                            g.dma_start(pg[:, b, 0:n, p * PAGE:(p + 1) * PAGE],
                                        src.rearrange("o p (n k) -> p (o n) k", n=n)).then_inc(s, 16)

                hold(g, seen)
                load_pages(0, 3, pages1_in)
                for i, c in enumerate(CHUNKS):
                    banks.wait_drained(g, l, f"p.{c}")
                    if i >= 2:
                        roped.wait(g, l, i - 1)
                    else:
                        g.wait_ge(roped.sem, l * roped.per + 1)
                    step(cosed, nc.gpsimd.tensor_tensor(ropecos[i % 2], q[c], cos, ALU.mult))
                    if c == "kb":
                        for n in range(NIDX):
                            k, p0 = n // 2, (n % 2) * HD
                            roped.wait(g, l, 2)
                            hold(g, seen)
                            step(padded, nc.gpsimd.tensor_copy(
                                diag(qpad_i, p0, HD, n * TS, TS),
                                q[f"qi{k}"][p0:p0 + HD, NP:T].rearrange("p (c b t) -> p c b t", b=2, t=TS)))
                for br in "ba":
                    roped.wait(g, l)
                    if br == "a":
                        banks.wait_full(g, l, "s4.1")
                    hold(g, seen)
                    for j in range(GQ):
                        step(padded, nc.gpsimd.tensor_copy(
                            diag(qpad, 0, 128, j * TS, TS),
                            q[f"q{br}{j}"][:, NP:T].rearrange("p (c b t) -> p c b t", b=2, t=TS)))
                banks.wait_full(g, l, "o4")
                hold(g, seen)
                load_pages(3, 2, pages2_in)

                xmix.wait(g, l)
                hold(g, seen)
                step(iotas, nc.gpsimd.iota(iota, [[1, SLOTS]], base=0, channel_multiplier=0,
                                        allow_small_or_imprecise_dtypes=True))
                step(iotas, nc.gpsimd.memset(xsort[:, :, SLOTS:SLOTP], 0.0))

                route.wait(g, l)
                for k in range(KD):
                    for hf in range(2):
                        banks.wait_drained(g, l, f"x{k}.{hf}")
                hold(g, seen)
                with g.Fori(0, N_EXP) as e:
                    first = g.value_load(table[0:1, 0, bass.ds(e, 1)], min_val=0, max_val=SLOTS)
                    nblk = g.value_load(table[0:1, 1, bass.ds(e, 1)], min_val=1, max_val=MAXBLK)
                    with g.Fori(0, nblk) as b:
                        n = g.snap(seen, min_val=0, max_val=200)
                        at = within(first + b * BLK)
                        g.wait_ge(gu_done, n + 1)
                        nc.gpsimd.tensor_copy(xs[:, :, :], xsort[:, :, bass.ds(at, BLK)]).then_inc(x_staged, 1)
                        g.wait_ge(x_staged, n + 1)
                        g.reg_add(seen, seen, 1)

        @block.tensor
        def _(pe):
            mm = nc.tensor.matmul
            for b in range(NBANK):
                pe.sem_inc(banks.drained[b], 1)
            pe.sem_inc(gu_done, 1)
            pe.wait_ge(start_in, 16 * 5)
            pe.wait_ge(silu_c, 1)
            pe.wait_ge(zeroed, 3)
            seen = pe.alloc_register("pe_blocks")
            pe.reg_mov(seen, 0)
            with pe.Fori(0, DEPTH) as l:
                issued = []

                def weights(pair):
                    pe.wait_ge(w_in[pair % RING], l * (ROUNDS * 16) + (pair // RING + 1) * 16)
                    return ring[:, pair % RING, :]

                def job(name):
                    assert PLAN[len(issued)] == name, (PLAN[len(issued)], name)
                    issued.append(name)
                    banks.wait_free(pe, l, name)
                    return banks.ap(name)

                def dense(out, w, rhs, stride=128, k0=0, n=KD):
                    for k in range(n):
                        last = mm(out, w[:, (k0 + k) * stride:(k0 + k) * stride + 128], rhs(k),
                                  start=(k == 0), stop=(k == n - 1))
                    return last

                def free_after(name):
                    banks.wait_full(pe, l, name)
                    pe.sem_inc(w_free, 1)

                for r in range(3):
                    ps = job(f"mod{r}")
                    for k in range(KD):
                        w = weights(P_ADA + r * KD + k)
                        for c in range(4):
                            last = mm(ps[32 * c:32 * c + 32, :], sc[:, k, :], w[:, c * 512:(c + 1) * 512],
                                      start=(k == 0), stop=(k == KD - 1), skip_group_check=True)
                        if k < KD - 1:
                            last.then_inc(w_free, 1)
                    banks.filled(last, f"mod{r}")
                    free_after(f"mod{r}")
                    ps = job(f"mt{r}")
                    banks.wait_drained(pe, l, f"mod{r}")
                    for j in range(4):
                        last = nc.tensor.transpose(ps[:, j * 128:(j + 1) * 128], mraw[r % 2][:, j * 128:(j + 1) * 128], ident)
                    banks.filled(last, f"mt{r}")

                def sum_squares(name, signal_n):
                    ps = job(name)
                    sq.wait(pe, l, signal_n)
                    for k in range(KD):
                        last = mm(ps[:, 0:T], ones, xsq[:, k, :], start=(k == 0), stop=(k == KD - 1))
                    banks.filled(last, name)

                sum_squares("ss1", 1)
                norm.wait(pe, l, 8)
                normed.wait(pe, l, 4)

                def project(c, w, t):
                    ps = job(f"p.{c}")
                    last = dense(ps[:, 0:T], w[:, t * 1024:(t + 1) * 1024], lambda k: h[:, k, :])
                    banks.filled(last, f"p.{c}")

                def rotate(c):
                    ps = job(f"r.{c}")
                    banks.wait_drained(pe, l, f"p.{c}")
                    banks.filled(mm(ps[:, 0:T], cs[:, C_ROT:C_ROT + 128], q[c], start=True, stop=True), f"r.{c}")

                def sample_scores(ps, qp, new_keys, part, p0, n):
                    hold(pe, seen)
                    for new in (True, False):
                        for odd in range(2):
                            for c in range(4):
                                b = 2 * c + odd
                                rhs = new_keys[p0:p0 + n, NP:T] if new else pg[p0:p0 + n, b, part, :]
                                last = mm(ps[32 * c:32 * c + 32, PAST:T] if new else ps[32 * c:32 * c + 32, 0:PAST],
                                          qp[p0:p0 + n, b, :], rhs, start=(odd == 0), stop=(odd == 1), skip_group_check=True)
                    return last

                w = weights(P_QI)
                project("qi0", w, 0)
                project("qi1", w, 1)
                rotate("qi0")
                free_after("p.qi1")
                w = weights(P_KW)
                project("ki", w, 0)
                rotate("qi1")
                ps = job("wi")
                for tb in range(3):
                    n = [128, 128, NS][tb]
                    for k in range(KD):
                        last = mm(ps[0:n, tb * 4:tb * 4 + 4], h[:, k, tb * 128:tb * 128 + n],
                                  w[:, 1024 + k * 4:1024 + k * 4 + 4], start=(k == 0), stop=(k == KD - 1))
                banks.filled(last, "wi")
                rotate("ki")
                free_after("wi")
                w = weights(P_KAB)
                project("ka", w, 0)
                project("kb", w, 1)
                rotate("ka")
                free_after("p.kb")

                ps = job("wrow")
                banks.wait_drained(pe, l, "wi")
                banks.filled(mm(ps[:, 0:4], cs[0:NS, C_ROW:C_ROW + 128], wi[0:NS, 2, :], start=True, stop=True), "wrow")
                for tb in range(2):
                    keys = 128 * (tb + 1)
                    for half in range(2):
                        name, p0 = f"L{tb}.{half}", half * HD
                        ps = job(name)
                        if tb == 0 and half == 0:
                            roped.wait(pe, l, 3)
                        for i in range(2):
                            last = mm(ps[:, i * keys:(i + 1) * keys], q[f"qi{i}"][p0:p0 + HD, tb * 128:(tb + 1) * 128],
                                      ki[p0:p0 + HD, 0:keys], start=True, stop=True)
                        banks.filled(last, name)
                ps = job("Ls")
                padded.wait(pe, l, 4)
                pe.wait_ge(pages1_in, (l + 1) * (16 * NB * PAGES))
                last = sample_scores(ps, qpad_i, ki, 2, 0, 128)
                banks.filled(last, "Ls")
                rotate("kb")
                w = weights(P_V)
                for tb in range(3):
                    n = [128, 128, NS][tb]
                    ps = job(f"v{tb}")
                    for k in range(KD):
                        last = mm(ps[0:n, 0:256], h[:, k, tb * 128:tb * 128 + n], w[:, k * 256:(k + 1) * 256],
                                  start=(k == 0), stop=(k == KD - 1))
                    banks.filled(last, f"v{tb}")
                free_after("v2")
                ps = job("score")
                banks.wait_drained(pe, l, "Ls")
                banks.filled(mm(ps[:, 0:T], cs[:, C_SUM:C_SUM + 128], idx[2], start=True, stop=True), "score")
                late = CHUNKS[5:]
                for i, c in enumerate(late):
                    if i % 2 == 0:
                        w = weights(P_QA + i // 2)
                    project(c, w, i % 2)
                    if i:
                        rotate(late[i - 1])
                    if i % 2:
                        free_after(f"p.{c}")
                rotate(late[-1])

                gates = [0]

                def gate_chunk():
                    n = gates[0]
                    if n == 16:
                        return
                    gates[0] += 1
                    w = weights(P_GATE + n // 2)
                    ps = job(f"g{n}")
                    last = dense(ps[:, 0:T], w[:, (n % 2) * 1024:(n % 2) * 1024 + 1024], lambda k: h[:, k, :])
                    banks.filled(last, f"g{n}")
                    if n % 2:
                        free_after(f"g{n}")

                def score_jobs(u):
                    br, tb, kv = UNITS[u]
                    kt = {"a": ka, "b": kb}[br]
                    if u == 0:
                        roped.wait(pe, l)
                    if tb < 2:
                        keys, p0 = unit_keys(u), kv * HD
                        for pair in range(2):
                            ps = job(f"s{u}.{pair}")
                            for i in range(2):
                                last = mm(ps[:, i * keys:(i + 1) * keys],
                                          q[f"q{br}{2 * pair + i}"][p0:p0 + HD, tb * 128:(tb + 1) * 128],
                                          kt[p0:p0 + HD, 0:keys], start=True, stop=True)
                            banks.filled(last, f"s{u}.{pair}")
                    else:
                        padded.wait(pe, l, 8 if br == "b" else 12)
                        if br == "a":
                            pe.wait_ge(pages2_in, (l + 1) * (16 * NB * PAGES))
                        for kv in range(2):
                            p0 = kv * HD
                            ps = job(f"s{u}.{kv}")
                            banks.filled(sample_scores(ps, qpad, kt, 0, p0, HD), f"s{u}.{kv}")

                def turn_jobs(u):
                    br, tb, kv = UNITS[u]
                    s = scores[u % 2]
                    if tb < 2:
                        s = s[:, 0:GQ * unit_keys(u)].rearrange("p (h k) -> p h k", h=GQ)
                        for n in range(turned(u)):
                            ps = job(f"t{u}.{n}")
                            if n == 0:
                                soft.wait(pe, l, soft_end(u))
                            for i in range(GQ):
                                last = nc.tensor.transpose(ps[:, i * 128:(i + 1) * 128], s[:, i, n * 128:(n + 1) * 128], ident)
                            banks.filled(last, f"t{u}.{n}")
                    else:
                        s = s[:, 0:2 * T].rearrange("p (g k) -> p g k", g=2)
                        ps = job(f"t{u}.0")
                        soft.wait(pe, l, soft_end(u))
                        for p in range(PAGES):
                            for kv in range(2):
                                last = nc.tensor.transpose(ps[:, (p * 2 + kv) * 128:(p * 2 + kv + 1) * 128],
                                                           s[:, kv, p * 128:(p + 1) * 128], ident)
                        banks.filled(last, f"t{u}.0")
                        ps = job(f"t{u}.1")
                        for kv in range(2):
                            last = nc.tensor.transpose(ps[0:NS, kv * 128:(kv + 1) * 128], s[:, kv, PAST:T], ident)
                        banks.filled(last, f"t{u}.1")

                def value_job(u):
                    br, tb, kv = UNITS[u]
                    v0 = 0 if br == "a" else 128
                    ps = job(f"o{u}")
                    for n in range(turned(u)):
                        banks.wait_drained(pe, l, f"t{u}.{n}")
                    if tb < 2:
                        p0 = kv * HD
                        for n in range(tb + 1):
                            last = mm(ps[p0:p0 + HD, :], v[:, n, v0 + p0:v0 + p0 + HD], probsT[:, n, :],
                                      start=(n == 0), stop=(n == tb))
                    else:
                        for kv in range(2):
                            p0 = kv * HD
                            mm(ps[p0:p0 + HD, 0:128], v[0:NS, 2, v0 + p0:v0 + p0 + HD], probsN[0:NS, kv * 128:(kv + 1) * 128],
                               start=True, stop=False, skip_group_check=True)
                            for b in range(NB):
                                for p in range(PAGES):
                                    c0 = (p * 2 + kv) * 128 + b * 16
                                    last = mm(ps[p0:p0 + HD, b * 16:(b + 1) * 16], pg[:, b, 1, p * 128 + p0:p * 128 + p0 + HD],
                                              probsT[:, :, :].rearrange("p a c -> p (a c)")[:, c0:c0 + 16],
                                              start=False, stop=(b == NB - 1 and p == PAGES - 1), skip_group_check=True)
                    banks.filled(last, f"o{u}")

                for i in range(len(UNITS) + 1):
                    if i < len(UNITS):
                        score_jobs(i)
                    gate_chunk()
                    if i:
                        turn_jobs(i - 1)
                    gate_chunk()
                    if i:
                        value_job(i - 1)

                for m in range(KD):
                    w = weights(P_PROJ + m // 2)[:, (m % 2) * 1024:(m % 2) * 1024 + 1024]
                    for half, c in enumerate("ab"):
                        ps = job(f"y{c}{m}")
                        if m == 0 and half == 0:
                            banks.wait_drained(pe, l, f"o{len(UNITS) - 1}")
                        last = dense(ps[:, 0:T], w, lambda k: yT[:, 4 * half + k, :], k0=4 * half, n=4)
                        banks.filled(last, f"y{c}{m}")
                    if m % 2:
                        free_after(f"yb{m}")
                for m in range(KD):
                    w = weights(P_OUT + m // 2)[:, (m % 2) * 1024:(m % 2) * 1024 + 1024]
                    ps = job(f"out{m}")
                    if m == 0:
                        merged.wait(pe, l)
                    banks.filled(dense(ps[:, 0:T], w, lambda k: gate[:, k, :]), f"out{m}")
                    if m % 2:
                        free_after(f"out{m}")

                sum_squares("ss2", 2)
                norm.wait(pe, l, 16)
                normed.wait(pe, l, 8)
                ps = job("router")
                for tb in range(3):
                    for k in range(KD):
                        last = mm(ps[0:TB, tb * 36:(tb + 1) * 36], h[:, k, tb * TB:(tb + 1) * TB],
                                  sm[:, S_WR + k * 36:S_WR + (k + 1) * 36], start=(k == 0), stop=(k == KD - 1))
                banks.filled(last, "router")
                for n in range(6):
                    ps = job(f"h{n}")
                    tb, k0 = n // 2, 4 * (n % 2)
                    for i in range(4):
                        last = nc.tensor.transpose(ps[0:TB, i * 128:(i + 1) * 128], h[:, k0 + i, tb * TB:(tb + 1) * TB], ident)
                    banks.filled(last, f"h{n}")
                ps = job("rank")
                route.wait(pe, l, R_HOT)
                hot = rt[9][:, 0:96].rearrange("p (t e) -> p t e", t=3)
                for tb in range(3):
                    for t2 in range(tb + 1):
                        wt = C_LOW if t2 == tb else C_ONE
                        mm(ps[0:TB, tb * 32:(tb + 1) * 32], cs[0:TB, wt:wt + TB], hot[0:TB, t2, :], start=(t2 == 0), stop=(t2 == tb))
                for tb in range(3):
                    last = mm(ps[:, 96:128], cs[0:TB, C_ONE:C_ONE + 128], hot[0:TB, tb, :], start=(tb == 0), stop=(tb == 2))
                banks.filled(last, "rank")
                for k in range(KD):
                    for hf in range(2):
                        ps = job(f"x{k}.{hf}")
                        if k == 0 and hf == 0:
                            route.wait(pe, l, R_SEL)
                            banks.wait_drained(pe, l, "h5")
                        for tb in range(3):
                            last = mm(ps[:, 0:T], hrow[0:TB, tb, k * 128:(k + 1) * 128], sel[0:TB, tb, hf * T:(hf + 1) * T],
                                      start=(tb == 0), stop=(tb == 2))
                        banks.filled(last, f"x{k}.{hf}")
                for s, (s0, ns) in enumerate(SB):
                    ps = job(f"c{s}")
                    if s == 0:
                        route.wait(pe, l)
                    hold(pe, seen)
                    for tb in range(3):
                        last = nc.tensor.transpose(ps[0:ns, tb * TB:(tb + 1) * TB], selw[0:TB, tb, s0:s0 + ns], ident[0:TB, 0:TB])
                    banks.filled(last, f"c{s}")
                hold(pe, seen)

                def turn_y(n):
                    pe.wait_ge(y_kept, n + 1)
                    pe.wait_ge(yt_kept, n + l + 1)
                    for i in range(2):
                        last = nc.tensor.transpose(pyt[:, i * 128:(i + 1) * 128], yb[:, i * 128:(i + 1) * 128], ident)
                    last.then_inc(yt_done, 1)

                with pe.Fori(0, N_EXP * 3 // RING) as er:
                    for j in range(RING // 3):
                        for s in range(3 * j, 3 * j + 3):
                            pe.wait_ge(w_in[s], l * (ROUNDS * 16) + er * 16 + (P_EXP // RING + 1) * 16)
                        hold(pe, seen)
                        nblk = pe.value_load(table[0:1, 1, bass.ds(er * (RING // 3) + j, 1)], min_val=1, max_val=MAXBLK)
                        w0, w1, wd = (ring[:, 3 * j + i, :] for i in range(3))
                        with pe.Fori(0, nblk) as b:
                            n = pe.snap(seen, min_val=0, max_val=200)
                            pe.wait_ge(x_staged, n + 1)
                            for k in range(KD):
                                c, w = k % 4, (w0, w1)[k // 4]
                                last = mm(pgu[32 * c:32 * c + 32, :], xs[:, k, :], w[:, c * 512:(c + 1) * 512],
                                          start=(k < 4), stop=(k >= 4), skip_group_check=True)
                            last.then_inc(gu_done, 1)
                            turn_y(n)
                            pe.wait_ge(gu_kept, n + 1)
                            for i in range(4):
                                last = nc.tensor.transpose(pgut[:, i * 128:(i + 1) * 128], gu[:, i * 128:(i + 1) * 128], ident)
                            last.then_inc(gut_done, 1)
                            pe.wait_ge(hdn_ready, n + 1)
                            for f in range(2):
                                for c in range(4):
                                    last = mm(py[32 * c:32 * c + 32, 0:256], hdn[:, f, :],
                                              wd[:, f * D + c * 256:f * D + (c + 1) * 256],
                                              start=(f == 0), stop=(f == 1), skip_group_check=True)
                            last.then_inc(y_done, 1)
                            pe.reg_add(seen, seen, 1)
                        pe.wait_ge(y_done, pe.snap(seen, min_val=1, max_val=200))
                        pe.sem_inc(w_free, 3)
                total = pe.snap(seen, min_val=1, max_val=200)
                turn_y(total)
                pe.wait_ge(yt_kept, total + l + 2)

                for s, (s0, ns) in enumerate(SB):
                    for hf in range(2):
                        ps = job(f"y{s}.{hf}")
                        hold(pe, seen)
                        for i in range(4):
                            last = nc.tensor.transpose(ps[0:ns, i * 128:(i + 1) * 128], ysort[:, 4 * hf + i, s0:s0 + ns], ident)
                        banks.filled(last, f"y{s}.{hf}")
                for m in range(KD):
                    ps = job(f"z{m}")
                    if m == 0:
                        for hf in range(2):
                            banks.wait_drained(pe, l, f"y{len(SB) - 1}.{hf}")
                    for s, (s0, ns) in enumerate(SB):
                        last = mm(ps[:, 0:T], yrow[0:ns, s, m * 128:(m + 1) * 128], comb[0:ns, s, :],
                                  start=(s == 0), stop=(s == len(SB) - 1))
                    banks.filled(last, f"z{m}")
                assert len(issued) == len(PLAN)

            pe.wait_ge(final_ss, 1)
            for k in range(KD):
                last = mm(pgu[:, 0:T], ones, xsq[:, k, :], start=(k == 0), stop=(k == KD - 1))
            last.then_inc(final_ss, 1)

        @block.scalar
        def _(a):
            act = nc.scalar.activation
            a.dma_start(cs[:, :], consts).then_inc(start_in, 16)
            a.dma_start(x[:, :, :], x_in).then_inc(start_in, 16)
            a.dma_start(sc[:, :, :], c_in).then_inc(start_in, 16)
            a.dma_start(gf[:, :], gfin).then_inc(start_in, 16)
            a.dma_start(ptab[:, :], page_table).then_inc(start_in, 16)
            a.sem_inc(yt_kept, 1)
            a.wait_ge(zeroed, 3)
            a.wait_ge(start_in, 16 * 5)
            act(sc[:, :, :], sc[:, :, :], ACT.Silu).then_inc(silu_c, 1)
            before = a.alloc_register("act_before")
            seen = a.alloc_register("act_blocks")
            a.reg_mov(seen, 0)
            with a.Fori(0, DEPTH) as l:
                def copy_out(name, out, src):
                    banks.wait_full(a, l, name)
                    banks.done(act(out, src, ACT.Copy), name)

                def norm_part(name, which):
                    banks.wait_drained(a, l, name)
                    root.up(act(rms[:, :], rms[:, :], ACT.Sqrt))
                    norm.wait(a, l, 8 * which + 2)
                    shift = (SH1, SH2)[which]
                    for k in range(4, KD):
                        normed.up(act(h[:, k, 0:NP], h[:, k, 0:NP], ACT.Identity, bias=mod[:, shift + k, 0:1],
                                      scale=gsc[:, which, k, 0:1]))

                a.wait_ge(xmoe.sem, l * xmoe.per + 1)
                for r in range(3):
                    copy_out(f"mod{r}", mraw[r % 2], banks.ap(f"mod{r}"))
                sq.up(act(xsq, x[:, :, :], ACT.Square))
                norm_part("ss1", 0)

                def raw(c):
                    copy_out(f"p.{c}", q[c], banks.ap(f"p.{c}")[:, 0:T])

                raw("qi0")
                raw("qi1")
                raw("ki")
                ps = banks.ap("wi")
                banks.wait_full(a, l, "wi")
                act(wi[:, 0:2, :], ps[:, 0:8].rearrange("p (t c) -> p t c", c=4), ACT.Copy)
                banks.done(act(wi[0:NS, 2, :], ps[0:NS, 8:12], ACT.Copy), "wi")
                raw("ka")
                raw("kb")
                for tb in range(2):
                    keys = 128 * (tb + 1)
                    relu = scores[tb][:, 0:NIDX * keys].rearrange("p (i h k) -> p h i k", i=2, h=2)
                    for half in range(2):
                        name = f"L{tb}.{half}"
                        banks.wait_full(a, l, name)
                        banks.done(act(relu[:, half, :, :], banks.ap(name)[:, 0:2 * keys].rearrange("p (i k) -> p i k", i=2),
                                       ACT.Relu), name)
                for tb in range(3):
                    n = [128, 128, NS][tb]
                    copy_out(f"v{tb}", v[0:n, tb, :], banks.ap(f"v{tb}")[0:n, 0:256])
                for c in CHUNKS[5:]:
                    raw(c)
                gates = [0]

                def gate_chunk():
                    n = gates[0]
                    if n == 16:
                        return
                    gates[0] += 1
                    banks.wait_full(a, l, f"g{n}")
                    banks.done(act(gate[:, n, :], banks.ap(f"g{n}")[:, 0:T], ACT.Sigmoid), f"g{n}")

                for i in range(len(UNITS) + 1):
                    gate_chunk()
                    if i:
                        u = i - 1
                        br, tb, kv = UNITS[u]
                        if tb < 2:
                            for n in range(turned(u)):
                                copy_out(f"t{u}.{n}", probsT[:, n, :], banks.ap(f"t{u}.{n}"))
                        else:
                            copy_out(f"t{u}.0", probsT[:, :, :].rearrange("p a c -> p (a c)")[:, 0:512], banks.ap(f"t{u}.0"))
                            copy_out(f"t{u}.1", probsN[0:NS, :], banks.ap(f"t{u}.1")[0:NS, 0:256])
                    if i < len(UNITS):
                        soft.wait(a, l, soft_end(i) - SOFT[i] + 2)
                        keys = unit_keys(i)
                        n = EXPS[i]
                        s = scores[i % 2][:, 0:n * keys].rearrange("p (h k) -> p h k", h=n)
                        for j in range(n):
                            exps.up(act(s[:, j, :], s[:, j, :], ACT.Exp, bias=stat[:, 1, j:j + 1], accum_out=stat[:, 2, j:j + 1]))
                    gate_chunk()
                    if i:
                        ps = banks.ap(f"o{u}")
                        y0 = 0 if br == "a" else 4
                        if tb < 2:
                            p0 = kv * HD
                            copy_out(f"o{u}", yT[p0:p0 + HD, y0:y0 + 4, tb * 128:(tb + 1) * 128],
                                     ps[p0:p0 + HD, :].rearrange("p (h t) -> p h t", h=4))
                        else:
                            copy_out(f"o{u}", by_seq(yT[:, y0:y0 + 4, NP:T], 4),
                                     ps[:, 0:128].rearrange("p (b h t) -> p h b t", b=NB, h=4))
                    if i == 6:
                        roped.wait(a, l)
                        banks.wait_drained(a, l, "v0")
                        banks.wait_drained(a, l, "v1")
                        banks.wait_drained(a, l, "v2")
                        for out, src in ((ka_out[l], ka[:, :]), (kb_out[l], kb[:, :]), (ki_out[l], ki[0:HD, :]),
                                         (vp_out[l].rearrange("n p c -> p n c"), v[:, 0:2, :]), (vs_out[l], v[0:NS, 2, :])):
                            a.dma_start(out, src).then_inc(rows_out, 16)

                xmix.wait(a, l)
                sq.up(act(xsq, x[:, :, :], ACT.Square))
                norm_part("ss2", 1)
                route.wait(a, l, 3)
                ex = rt[2][0:TB, 0:12]
                rexp.up(act(ex, rt[1][0:TB, 0:12], ACT.Exp))
                for n in range(6):
                    copy_out(f"h{n}", hrow[0:TB, n // 2, (n % 2) * 512:(n % 2 + 1) * 512], banks.ap(f"h{n}")[0:TB, :])
                route.wait(a, l, R_GAP)
                rexp.up(act(dest[0:TB, 6, :], dest[0:TB, 5, :], ACT.Exp))
                for k in range(KD):
                    for hf in range(2):
                        copy_out(f"x{k}.{hf}", xsort[:, k, hf * T:(hf + 1) * T], banks.ap(f"x{k}.{hf}")[:, 0:T])
                def keep_y(n):
                    a.wait_ge(yt_done, n + l + 1)
                    a.wait_ge(yt_kept, n + l + 1)
                    at = a.snap(before, min_val=0, max_val=SLOTS)
                    act(ysort[:, :, bass.ds(at, BLK)].rearrange("p (c i) s -> p c i s", i=2),
                        pyt[:, 0:256].rearrange("p (i c s) -> p c i s", i=2, c=4), ACT.Copy).then_inc(yt_kept, 1)

                for s, (s0, ns) in enumerate(SB):
                    copy_out(f"c{s}", comb[0:ns, s, :], banks.ap(f"c{s}")[0:ns, 0:T])

                a.reg_mov(before, SLOTS)
                with a.Fori(0, N_EXP) as e:
                    first = a.value_load(table[0:1, 0, bass.ds(e, 1)], min_val=0, max_val=SLOTS)
                    nblk = a.value_load(table[0:1, 1, bass.ds(e, 1)], min_val=1, max_val=MAXBLK)
                    with a.Fori(0, nblk) as b:
                        n = a.snap(seen, min_val=0, max_val=200)
                        a.wait_ge(gu_done, n + 2)
                        act(gu, pgu[:, :], ACT.Copy).then_inc(gu_kept, 1)
                        keep_y(n)
                        a.wait_ge(summed, n + 1)
                        act(sg, gusum[:, 0:2, :], ACT.Silu).then_inc(silu_done, 1)
                        a.reg_mov(before, within(first + b * BLK))
                        a.reg_add(seen, seen, 1)
                keep_y(a.snap(seen, min_val=1, max_val=200))
                for s, (s0, ns) in enumerate(SB):
                    copy_out(f"y{s}.0", yrow[0:ns, s, 0:512], banks.ap(f"y{s}.0")[0:ns, :])
                a.wait_ge(rows_out, (l + 1) * (16 * 5))

            a.wait_ge(xmoe.sem, DEPTH * xmoe.per + 1)
            act(xsq, x[:, :, :], ACT.Square).then_inc(final_ss, 1)
            a.wait_ge(final, 1)
            act(rms[:, :], rms[:, :], ACT.Sqrt).then_inc(final_rt, 1)
            a.wait_ge(final, 3 + KD)
            a.dma_start(y_out, h[:, :, :]).then_inc(y_stored, 16)
            a.wait_ge(y_stored, 16)
            a.wait_ge(rows_out, DEPTH * 16 * 5)

        @block.vector
        def _(d):
            V = nc.vector
            d.sem_inc(roped.sem, 1)
            d.sem_inc(xmoe.sem, 1)
            d.sem_inc(y_kept, 1)
            d.wait_ge(start_in, 16 * 5)
            seen = d.alloc_register("dve_blocks")
            d.reg_mov(seen, 0)
            with d.Fori(0, DEPTH) as l:
                def vnorm(name, which, gain, shift):
                    banks.wait_full(d, l, name)
                    banks.done(V.tensor_scalar(rms[:, :], banks.ap(name)[:, 0:T], 1.0 / D, EPS, ALU.mult, ALU.add), name)
                    root.wait(d, l, which + 1)
                    norm.up(V.reciprocal(rms[:, :], rms[:, :]))
                    norm.wait_so_far(d, l)
                    norm.up(V.tensor_tensor(h[:, :, :], x[:, :, :], bc(rms[:, :].unsqueeze(1), [128, KD, T]), ALU.mult))
                    norm.wait_so_far(d, l)
                    for k in range(4):
                        norm.up(V.tensor_scalar(h[:, k, 0:NP], h[:, k, 0:NP], gsc[:, which, k, 0:1], mod[:, shift + k, 0:1],
                                                ALU.mult, ALU.add))
                    hs = by_seq(h[:, :, NP:T], KD)
                    shape = [128, KD, NB, TS]
                    norm.up(V.tensor_tensor(hs, hs, bc(gsc[:, which, :, 1:NCOND].unsqueeze(3), shape), ALU.mult))
                    norm.wait_so_far(d, l)
                    norm.up(V.tensor_tensor(hs, hs, bc(mod[:, shift:shift + KD, 1:NCOND].unsqueeze(3), shape), ALU.add))

                d.wait_ge(small_in, (l + 1) * 16)
                for r in range(3):
                    shape = [128, 4, 4, NCOND]
                    banks.wait_full(d, l, f"mt{r}")
                    banks.done(V.tensor_tensor(
                        mod[:, r * 16:(r + 1) * 16, :].rearrange("p (c j) n -> p c j n", c=4),
                        banks.ap(f"mt{r}").rearrange("p (j c n) -> p c j n", j=4, c=4)[:, :, :, 0:NCOND],
                        bc(sm[:, S_BA + r * 16:S_BA + (r + 1) * 16].rearrange("p (c j) -> p c j", c=4).unsqueeze(3), shape),
                        ALU.add), f"mt{r}")
                for r in range(3):
                    banks.wait_drained(d, l, f"mt{r}")
                for i, (g0, s0) in enumerate(((S_GM, SC1), (S_GF, SC2))):
                    mods.up(V.scalar_tensor_tensor(gsc[:, i, :, :], mod[:, s0:s0 + KD, :], 1.0,
                                                   bc(sm[:, g0:g0 + KD].unsqueeze(2), [128, KD, NCOND]), ALU.add, ALU.mult))
                mods.wait_so_far(d, l)
                vnorm("ss1", 0, S_GM, SH1)

                def rope(c):
                    banks.wait_full(d, l, f"r.{c}")
                    ps = banks.ap(f"r.{c}")[:, 0:T]
                    roped.wait_so_far(d, l)
                    banks.done(V.tensor_tensor(rot, ps, sin, ALU.mult), f"r.{c}")
                    banks.wait_drained(d, l, f"r.{c}")
                    i = roped.n
                    cosed.wait(d, l, i + 1)
                    roped.up(V.tensor_tensor(q[c], ropecos[i % 2], rot, ALU.add))

                def step(ins):
                    ix.up(ins)
                    ix.wait_so_far(d, l)

                def select():
                    for tb in range(3):
                        keys = [128, 256, T][tb]
                        seen_keys = picked[:, 0:keys]
                        for r in range(KEEP_P // 8):
                            src = seen_keys if r else idx[tb]
                            hold(d, seen)
                            step(V.max(top[:, :], src))
                            hold(d, seen)
                            step(V.match_replace(seen_keys, top[:, :], src, -3.0e38))
                            yield
                        b = bias_a[tb]
                        if tb == 2:
                            hold(d, seen)
                            step(V.max(top[:, :], seen_keys))
                            step(V.scalar_tensor_tensor(b, seen_keys, top[:, 0:1], cs[:, C_REV:C_REV + T], ALU.is_ge, ALU.mult))
                            step(V.tensor_reduce(top[:, 0:1], b, AX, ALU.max))
                            step(V.tensor_scalar(b, b, top[:, 0:1], None, ALU.is_equal))
                            step(V.tensor_tensor(seen_keys, seen_keys, idx[tb], ALU.is_equal))
                            step(V.tensor_tensor(b, seen_keys, b, ALU.subtract))
                        else:
                            step(V.tensor_tensor(b, seen_keys, idx[tb], ALU.is_equal))
                        step(V.scalar_tensor_tensor(b, b, OFF, cbias[tb], ALU.mult, ALU.add))
                        yield

                rot = carve(9024, T)
                for c in ("qi0", "qi1", "ki", "ka"):
                    rope(c)
                ps = banks.ap("wrow")
                banks.wait_full(d, l, "wrow")
                banks.done(V.tensor_tensor(wrow[:, 0:4], ps[:, 0:4], cs[:, C_HEAD:C_HEAD + 4], ALU.mult), "wrow")
                banks.wait_drained(d, l, "wrow")
                step(V.tensor_reduce(wrow[:, 4:5], wrow[:, 0:4], AX, ALU.add))
                banks.wait_drained(d, l, "wi")
                for tb in range(2):
                    keys = 128 * (tb + 1)
                    banks.wait_drained(d, l, f"L{tb}.0")
                    banks.wait_drained(d, l, f"L{tb}.1")
                    for n in range(NIDX):
                        step(V.scalar_tensor_tensor(idx[tb], scores[tb][:, n * keys:(n + 1) * keys], wi[:, tb, n:n + 1],
                                                    idx[tb] if n else cbias[tb], ALU.mult, ALU.add))
                banks.wait_full(d, l, "Ls")
                banks.done(V.tensor_scalar(idx[2], banks.ap("Ls")[:, 0:T], 0.0, wrow[:, 4:5], ALU.max, ALU.mult), "Ls")
                rope("kb")
                banks.wait_full(d, l, "score")
                banks.done(V.tensor_tensor(idx[2], banks.ap("score")[:, 0:T], cbias[2], ALU.add), "score")
                banks.wait_drained(d, l, "score")
                selection = select()
                for c in CHUNKS[5:]:
                    rope(c)
                    for _ in range(3):
                        next(selection, None)
                for _ in selection:
                    pass

                for u, (br, tb, kv) in enumerate(UNITS):
                    keys, n = unit_keys(u), EXPS[u]
                    s = scores[u % 2][:, 0:n * keys].rearrange("p (h k) -> p h k", h=n)
                    bias = (cbias if br == "b" else bias_a)[tb]
                    for i in range(2):
                        w = n // 2
                        banks.wait_full(d, l, f"s{u}.{i}")
                        banks.done(V.scalar_tensor_tensor(
                            s[:, i * w:(i + 1) * w, :], banks.ap(f"s{u}.{i}")[:, 0:w * keys].rearrange("p (h k) -> p h k", h=w),
                            SCALE, bc(bias.unsqueeze(1), [128, w, keys]), ALU.mult, ALU.add), f"s{u}.{i}")
                    banks.wait_drained(d, l, f"s{u}.0")
                    banks.wait_drained(d, l, f"s{u}.1")
                    if u:
                        soft.wait_so_far(d, l)
                    soft.up(V.tensor_reduce(stat[:, 0, 0:n], s, AX, ALU.max))
                    soft.wait_so_far(d, l)
                    soft.up(V.tensor_scalar(stat[:, 1, 0:n], stat[:, 0, 0:n], -1.0, None, ALU.mult))
                    exps.wait(d, l, sum(EXPS[:u + 1]))
                    soft.up(V.reciprocal(stat[:, 3, 0:n], stat[:, 2, 0:n]))
                    soft.wait_so_far(d, l)
                    for j in range(n):
                        soft.up(V.tensor_scalar(s[:, j, :], s[:, j, :], stat[:, 3, j:j + 1], None, ALU.mult))

                for m in range(KD):
                    for half, c in enumerate("ab"):
                        banks.wait_drained(d, l, f"g{8 * half + m}")
                        banks.wait_full(d, l, f"y{c}{m}")
                        gm = gate[:, 8 * half + m, :]
                        banks.done(V.tensor_tensor(gm, gm, banks.ap(f"y{c}{m}")[:, 0:T], ALU.mult), f"y{c}{m}")
                    banks.wait_drained(d, l, f"ya{m}")
                    banks.wait_drained(d, l, f"yb{m}")
                    merged.up(V.tensor_tensor(gate[:, m, :], gate[:, m, :], gate[:, 8 + m, :], ALU.add))

                def add_gated(name, m, gt, signal):
                    ps = banks.ap(name)
                    banks.wait_full(d, l, name)
                    if m:
                        signal.wait_so_far(d, l)
                    xtmp.up(V.tensor_tensor(tmp4, ps[:, NP:T].rearrange("p (b t) -> p b t", t=TS),
                                            bc(mod[:, gt + m, 1:NCOND].unsqueeze(2), [128, NB, TS]), ALU.mult))
                    banks.done(V.scalar_tensor_tensor(x[:, m, 0:NP], ps[:, 0:NP], mod[:, gt + m, 0:1], x[:, m, 0:NP],
                                                      ALU.mult, ALU.add), name)
                    xtmp.wait_so_far(d, l)
                    signal.up(V.tensor_tensor(x[:, m, NP:T], x[:, m, NP:T], rms[:, 0:NS], ALU.add))

                tmp4 = rms[:, 0:NS].rearrange("p (b t) -> p b t", t=TS)
                for m in range(KD):
                    add_gated(f"out{m}", m, GT1, xmix)

                xmix.wait_so_far(d, l)
                vnorm("ss2", 1, S_GF, SH2)

                def r(ins):
                    route.up(ins)
                    route.wait_so_far(d, l)

                def trio(i):
                    return dest[0:TB, i, :]

                def spread(ap, n):
                    return bc(ap.unsqueeze(2), [TB, 3, n])

                def first_best(vals, best, out, n, tmp):
                    r(V.tensor_reduce(best, vals, AX, ALU.max))
                    r(V.tensor_tensor(tmp, vals, spread(best, n), ALU.subtract))
                    r(V.scalar_tensor_tensor(out, tmp, 0.0, bc(cs[0:TB, C_REV:C_REV + n].unsqueeze(1), [TB, 3, n]),
                                             ALU.is_ge, ALU.mult))
                    r(V.tensor_reduce(trio(4), out, AX, ALU.max))
                    r(V.tensor_tensor(out, out, spread(trio(4), n), ALU.is_equal))

                lg = rt[0][0:TB, 0:108].rearrange("p (t c) -> p t c", t=3)
                d4, e4, g4 = (rt[i][0:TB, 0:12].rearrange("p (t c) -> p t c", t=3) for i in (1, 2, 3))
                le, d32, hot1, hot2, tmp32, hot = (rt[i][0:TB, 0:96].rearrange("p (t c) -> p t c", t=3) for i in (4, 5, 6, 7, 8, 9))
                banks.wait_full(d, l, "router")
                banks.done(V.tensor_tensor(lg, banks.ap("router")[0:TB, 0:108].rearrange("p (t c) -> p t c", t=3),
                                           bc(sm[0:TB, S_BR:S_BR + 36].unsqueeze(1), [TB, 3, 36]), ALU.add), "router")
                banks.wait_drained(d, l, "router")
                first_best(lg[:, :, 0:4], trio(0), g4, 4, d4)
                r(V.tensor_scalar(g4, g4, -1.0, -OFF, ALU.add, ALU.mult))
                le4 = rt[4][0:TB, 0:96].rearrange("p (t g e) -> p t g e", t=3, g=N_GRP)
                for tb in range(3):
                    route.up(V.tensor_tensor(le4[:, tb], lg[:, tb, 4:36].rearrange("p (g e) -> p g e", g=N_GRP),
                                             bc(g4[:, tb, :].unsqueeze(2), [TB, N_GRP, 8]), ALU.add))
                route.wait_so_far(d, l)
                first_best(le, trio(1), hot1, N_EXP, d32)
                r(V.scalar_tensor_tensor(tmp32, hot1, 3.0 * OFF, le, ALU.mult, ALU.add))
                first_best(tmp32, trio(2), hot2, N_EXP, d32)
                r(V.tensor_tensor(hot, hot1, hot2, ALU.add))
                assert route.n == R_HOT, route.n
                r(V.tensor_tensor(trio(5), trio(2), trio(1), ALU.subtract))
                assert route.n == R_GAP, route.n
                banks.wait_full(d, l, "rank")
                ps = banks.ap("rank")
                r(V.tensor_copy(cnt[:, 0, :], ps[:, 96:128]))
                r(V.tensor_tensor_scan(cnt[:, 1, :], cs[:, C_ONE:C_ONE + N_EXP], cnt[:, 0, :], 0.0, ALU.mult, ALU.add))
                r(V.tensor_tensor(cnt[:, 1, :], cnt[:, 1, :], cnt[:, 0, :], ALU.subtract))
                banks.done(V.tensor_tensor(d32, ps[0:TB, 0:96].rearrange("p (t c) -> p t c", t=3),
                                           bc(cnt[0:TB, 1, :].unsqueeze(1), [TB, 3, N_EXP]), ALU.add), "rank")
                banks.wait_drained(d, l, "rank")
                for i, oh in ((9, hot1), (10, hot2)):
                    r(V.tensor_tensor(tmp32, oh, d32, ALU.mult))
                    r(V.tensor_reduce(trio(i), tmp32, AX, ALU.add))
                iotas.wait(d, l)
                for tb in range(3):
                    route.up(V.tensor_scalar(sel[0:TB, tb, :], iota[0:TB, :], dest[0:TB, 9, tb:tb + 1], None, ALU.is_equal))
                route.wait_so_far(d, l)
                for tb in range(3):
                    route.up(V.scalar_tensor_tensor(sel[0:TB, tb, :], iota[0:TB, :], dest[0:TB, 10, tb:tb + 1], sel[0:TB, tb, :],
                                                    ALU.is_equal, ALU.add))
                assert route.n == R_SEL, route.n
                r(V.tensor_copy(table[:, 0, :], cnt[0:1, 1, :]))
                r(V.tensor_scalar(cnt[0:1, 2, :], cnt[0:1, 0, :], BLK + 0.5, 1.0, ALU.is_ge, ALU.add))
                for n in range(2, MAXBLK):
                    r(V.scalar_tensor_tensor(cnt[0:1, 2, :], cnt[0:1, 0, :], n * BLK + 0.5, cnt[0:1, 2, :], ALU.is_ge, ALU.add))
                r(V.tensor_copy(table[:, 1, :], cnt[0:1, 2, :]))
                rexp.wait(d, l, 1)
                r(V.tensor_reduce(trio(3), e4, AX, ALU.add))
                rexp.wait(d, l)
                r(V.scalar_tensor_tensor(trio(3), trio(6), 1.0, trio(3), ALU.add, ALU.mult))
                r(V.reciprocal(trio(7), trio(3)))
                r(V.tensor_tensor(trio(8), trio(7), trio(6), ALU.mult))
                for tb in range(3):
                    r(V.tensor_scalar(selw[0:TB, tb, :], iota[0:TB, :], dest[0:TB, 9, tb:tb + 1], dest[0:TB, 7, tb:tb + 1],
                                      ALU.is_equal, ALU.mult))
                    r(V.tensor_scalar(eq1[0:TB, :], iota[0:TB, :], dest[0:TB, 10, tb:tb + 1], dest[0:TB, 8, tb:tb + 1],
                                      ALU.is_equal, ALU.mult))
                    r(V.tensor_tensor(selw[0:TB, tb, :], selw[0:TB, tb, :], eq1[0:TB, :], ALU.add))

                hold(d, seen)
                with d.Fori(0, N_EXP) as e:
                    nblk = d.value_load(table[0:1, 1, bass.ds(e, 1)], min_val=1, max_val=MAXBLK)
                    with d.Fori(0, nblk) as b:
                        n = d.snap(seen, min_val=0, max_val=200)
                        d.wait_ge(gut_done, n + 1)
                        V.tensor_reduce(gusum, pgut[:, :].rearrange("p (i c s) -> p i s c", i=4, c=4), AX, ALU.add).then_inc(summed, 1)
                        d.wait_ge(summed, n + 1)
                        d.wait_ge(silu_done, n + 1)
                        V.tensor_tensor(hdn, sg, gusum[:, 2:4, :], ALU.mult).then_inc(hdn_ready, 1)
                        d.wait_ge(y_done, n + 1)
                        V.tensor_copy(yb[:, :], py[:, 0:256]).then_inc(y_kept, 1)
                        d.reg_add(seen, seen, 1)
                for s, (s0, ns) in enumerate(SB):
                    banks.wait_full(d, l, f"y{s}.1")
                    banks.done(V.tensor_copy(yrow[0:ns, s, 512:1024], banks.ap(f"y{s}.1")[0:ns, :]), f"y{s}.1")
                for m in range(KD):
                    add_gated(f"z{m}", m, GT2, xmoe)
                for s in (mods, norm, roped, ix, soft, merged, xmix, route, xmoe, xtmp):
                    assert s.n == s.per, (s.sem.name, s.n, s.per)

            d.wait_ge(final_ss, 2)
            V.tensor_scalar(rms[:, :], pgu[:, 0:T], 1.0 / D, EPS, ALU.mult, ALU.add).then_inc(final, 1)
            d.wait_ge(final_rt, 1)
            V.reciprocal(rms[:, :], rms[:, :]).then_inc(final, 1)
            d.wait_ge(final, 2)
            V.tensor_tensor(h[:, :, :], x[:, :, :], bc(rms[:, :].unsqueeze(1), [128, KD, T]), ALU.mult).then_inc(final, 1)
            d.wait_ge(final, 3)
            for k in range(KD):
                V.tensor_scalar(h[:, k, :], h[:, k, :], gf[:, k:k + 1], None, ALU.mult).then_inc(final, 1)



def constants():
    c = np.zeros((128, C_END), np.float32)
    p = np.arange(128)
    c[:, C_ID:C_ID + 128] = np.eye(128)
    for i in range(128):
        if i % HD < HD // 2:
            c[i + HD // 2, C_ROT + i] = -1.0
        else:
            c[i - HD // 2, C_ROT + i] = 1.0
    c[:, C_ONE:C_ONE + 128] = 1.0
    c[:, C_LOW:C_LOW + 128] = p[:, None] < p[None, :]
    seq, head, tok = p // 16, (p // 4) % 4, p % 4
    c[:, C_SUM:C_SUM + 128] = (seq[:, None] == seq[None]) & (tok[:, None] == tok[None])
    for r in range(128):
        c[seq[r] * 4 + tok[r], C_ROW + r] = 1.0
        c[r, C_HEAD + head[r]] = 1.0
    pos = np.concatenate([np.arange(NP), PAST + np.tile(np.arange(TS), NB)]).astype(np.float32)
    half = HD // 2
    inv = np.power(np.float32(10000.0), -np.arange(half, dtype=np.float32) / np.float32(half)).astype(np.float32)
    ang = pos[None, :] * inv[p % half][:, None]
    c[:, C_COS:C_COS + T] = np.cos(ang)
    c[:, C_SIN:C_SIN + T] = np.sin(ang)
    c[:, C_CB0:C_CB0 + 128] = np.where(p[None] <= p[:, None], 0.0, OFF)
    c[:, C_CB1:C_CB1 + 256] = np.where(np.arange(256)[None] <= 128 + p[:, None], 0.0, OFF)
    s = np.arange(NS)
    ok = (s[None] // TS == seq[:, None]) & (s[None] % TS <= tok[:, None])
    c[:, C_SM + PAST:C_SM + T] = np.where(ok, 0.0, OFF)
    c[:, C_REV:C_REV + T] = T - np.arange(T)
    return c


def kernel(x_prompt, x_sample, c_prompt, c_sample, cache_k_a, cache_v_a, cache_idx_k, cache_k_b, cache_v_b,
           page_table, w_ada, b_ada, g_mix, w_in, w_proj_a, w_proj_b, w_out, g_ffn, w_router_group,
           b_router_group, w_router_expert, b_router_expert, w_exp_gate, w_exp_up, w_exp_down, g_final):
    import concourse.bacc as bacc
    from concourse.bass_utils import run_bass_kernel_spmd as run

    def arr(a):
        return np.asarray(a)

    def cols(w):
        return w.reshape(-1, 128, w.shape[-1]).transpose(1, 0, 2)

    xt = np.concatenate([arr(x_prompt).reshape(NP, D), arr(x_sample).reshape(NS, D)]).T
    ct = np.concatenate([arr(c_prompt), arr(c_sample), np.zeros((32 - NCOND, D), np.float32)]).T
    x_l, c_l = np.ascontiguousarray(cols(xt)), np.ascontiguousarray(cols(ct))

    ws = np.zeros((DEPTH, PAIRS, 128, PAIR), np.float32)
    win = arr(w_in)
    at = np.cumsum([0, 512, 128, 128, 256, 64, 4, 512, 128, 128, 1024, 1024])
    QA, KA, VA, QI, KI, WI, QB, KB, VB, GA, GB = (slice(at[i], at[i + 1]) for i in range(11))
    heads = [np.concatenate([np.arange(64 * j, 64 * j + 64), np.arange(64 * (j + 4), 64 * (j + 4) + 64)]) for j in range(4)]

    def put(l, pair, t, w):
        w = cols(w)
        ws[l, pair, :, t * 1024:t * 1024 + w.shape[1] * w.shape[2]] = w.reshape(128, -1)

    for l in range(DEPTH):
        ws[l, P_ADA:P_ADA + 24] = arr(w_ada)[l].reshape(KD, 128, 3, PAIR).transpose(2, 0, 1, 3).reshape(24, 128, PAIR)
        wl = win[l]
        put(l, P_QI, 0, wl[:, QI][:, :128])
        put(l, P_QI, 1, wl[:, QI][:, 128:])
        put(l, P_KW, 0, np.concatenate([wl[:, KI], wl[:, KI]], axis=1))
        put(l, P_KW, 1, wl[:, WI])
        put(l, P_KAB, 0, wl[:, KA])
        put(l, P_KAB, 1, wl[:, KB])
        put(l, P_V, 0, np.concatenate([wl[:, VA], wl[:, VB]], axis=1))
        for j in range(4):
            put(l, P_QA + j // 2, j % 2, wl[:, QA][:, heads[j]])
            put(l, P_QB + j // 2, j % 2, wl[:, QB][:, heads[j]])
        for m in range(8):
            part = slice(m * 128, (m + 1) * 128)
            put(l, P_GATE + m // 2, m % 2, wl[:, GA][:, part])
            put(l, P_GATE + 4 + m // 2, m % 2, wl[:, GB][:, part])
            put(l, P_PROJ + m // 2, m % 2, np.concatenate([arr(w_proj_a)[l][heads[j]][:, part] for j in range(4)]
                                                          + [arr(w_proj_b)[l][heads[j]][:, part] for j in range(4)]))
            put(l, P_OUT + m // 2, m % 2, arr(w_out)[l][:, part])
        for e in range(N_EXP):
            both = np.concatenate([arr(w_exp_gate)[l, e], arr(w_exp_up)[l, e]], axis=1)
            put(l, P_EXP + 3 * e, 0, both[:D // 2])
            put(l, P_EXP + 3 * e + 1, 0, both[D // 2:])
            put(l, P_EXP + 3 * e + 2, 0, arr(w_exp_down)[l, e])
    ws = ws.reshape(DEPTH * PAIRS, 128, PAIR)

    sm = np.zeros((DEPTH, 128, S_END), np.float32)
    for l in range(DEPTH):
        wr = np.concatenate([arr(w_router_group)[l], arr(w_router_expert)[l]], axis=1)
        sm[l, :, S_WR:S_WR + KD * 36] = cols(wr).reshape(128, -1)
        sm[l, :, S_GM:S_GM + KD] = arr(g_mix)[l].reshape(KD, 128).T
        sm[l, :, S_GF:S_GF + KD] = arr(g_ffn)[l].reshape(KD, 128).T
        sm[l, :, S_BA:S_BA + NMOD] = arr(b_ada)[l].reshape(NMOD, 128).T
        sm[l, :, S_BR:S_BR + 4] = arr(b_router_group)[l][None]
        sm[l, :, S_BR + 4:S_BR + 36] = arr(b_router_expert)[l][None]

    def keys_across(a):
        return arr(a).reshape(DEPTH * POOL, PAGE, -1).transpose(0, 2, 1)

    kip = keys_across(cache_idx_k)
    pages = np.ascontiguousarray(np.concatenate(
        [keys_across(cache_k_b), arr(cache_v_b).reshape(DEPTH * POOL, PAGE, 128), np.concatenate([kip, kip], axis=1),
         keys_across(cache_k_a), arr(cache_v_a).reshape(DEPTH * POOL, PAGE, 128)], axis=2))

    ins = {"wstream": ws, "small": sm, "consts": constants(), "pages": pages,
           "page_table": np.ascontiguousarray(arr(page_table).reshape(1, NB * PAGES)), "x_in": x_l, "c_in": c_l,
           "gfin": np.ascontiguousarray(arr(g_final).reshape(KD, 128).T)}
    outs = {"y": (128, KD, T), "ka": (DEPTH, 128, T), "kb": (DEPTH, 128, T), "ki": (DEPTH, HD, T),
            "vp": (DEPTH, 2, 128, 256), "vs": (DEPTH, NS, 256)}
    nc = bacc.Bacc("TRN2", target_bir_lowering=False, num_devices=1, dynamic_dma_scratch_size=4096)
    i = {n: nc.dram_tensor(n, a.shape, mybir.dt.from_np(a.dtype), kind="ExternalInput").ap() for n, a in ins.items()}
    o = {n: nc.dram_tensor("out_" + n, s, F32, kind="ExternalOutput").ap() for n, s in outs.items()}
    decoder_trunk(nc, i["wstream"], i["small"], i["consts"], i["pages"], i["page_table"], i["x_in"], i["c_in"], i["gfin"],
                  o["y"], o["ka"], o["kb"], o["ki"], o["vp"], o["vs"])
    r = run(nc, [ins], core_ids=[0]).results[0]
    g = {n: np.asarray(r["out_" + n]) for n in outs}

    y = g["y"].transpose(2, 1, 0).reshape(T, D)

    def rows(a):
        return a.transpose(0, 2, 1)

    def prompt(a):
        return np.ascontiguousarray(a[:, :NP]).reshape(DEPTH, 1, NP, -1)

    def sample(a):
        return np.ascontiguousarray(a[:, NP:]).reshape(DEPTH, NB, TS, -1)

    vv = np.concatenate([g["vp"].reshape(DEPTH, NP, 256), g["vs"]], axis=1)
    parts = [rows(g["ka"]), vv[..., :128], rows(g["kb"]), vv[..., 128:], rows(g["ki"])]

    def by_head(a, i):
        return a.reshape(a.shape[:3] + (NKV, HD)) if i < 4 else a

    return (np.ascontiguousarray(y[:NP]).reshape(1, NP, D), np.ascontiguousarray(y[NP:]).reshape(NB, TS, D),
            *(by_head(prompt(a), i) for i, a in enumerate(parts)), *(by_head(sample(a), i) for i, a in enumerate(parts)))
```

```python
from contextlib import ExitStack

import concourse.bass as bass
import numpy as np
from concourse import mybir

F32 = mybir.dt.float32
I32 = mybir.dt.int32
ALU = mybir.AluOpType
ACT = mybir.ActivationFunctionType
AX = mybir.AxisListType.X

D = 1024
DEPTH = 2
NP, NB, TS = 256, 8, 4
NS = NB * TS
T = NP + NS
PAGE, PAGES, POOL = 128, 2, 20
PAST = PAGE * PAGES
HD = 64
NH, NKV, GQ = 8, 2, 4
NIDX = 4
N_EXP, D_EXP, N_GRP = 32, 256, 4
KEEP_P, KEEP_S = 64, 65
EPS = 1e-6
SCALE = HD ** -0.5
OFF = -1.0e30

KD = D // 128
NCOND = 1 + NB
NMOD = 6 * KD
SH1, SC1, GT1, SH2, SC2, GT2 = (i * KD for i in range(6))

PAIR = 2048
RING = 12
PAIRS = 144
ROUNDS = PAIRS // RING
P_MOD0 = 0
P_QI, P_KW, P_KAB, P_V, P_QA, P_QB, P_GATE = 8, 9, 10, 11, 12, 14, 16
P_MOD1, P_MOD2 = 24, 32
P_PROJ, P_OUT, P_EXP = 40, 44, 48

TB = T // 3
SLOTS = 2 * T
BLK = 32
MAXBLK = T // BLK
SLOTP = SLOTS + BLK
SB = [(i * 128, min(128, SLOTS - i * 128)) for i in range((SLOTS + 127) // 128)]

C_ID, C_ROT, C_ONE, C_LOW, C_SUM, C_ROW = (i * 128 for i in range(6))
C_HEAD = 768
C_COS = C_HEAD + 4
C_SIN = C_COS + T
C_CB0 = C_SIN + T
C_CB1 = C_CB0 + 128
C_SM = C_CB1 + 256
C_REV = C_SM + T
C_END = C_REV + T

S_WR = 0
S_GM = S_WR + KD * 36
S_GF = S_GM + KD
S_BA = S_GF + KD
S_BR = S_BA + NMOD
S_END = S_BR + 36

CHUNKS = ["qi0", "qi1", "ki", "ka", "kb"] + [f"qa{i}" for i in range(4)] + [f"qb{i}" for i in range(4)]
UNITS = [("b", 0, 0), ("b", 0, 1), ("b", 1, 0), ("b", 1, 1), ("b", 2, 0),
         ("a", 0, 0), ("a", 0, 1), ("a", 1, 0), ("a", 1, 1), ("a", 2, 0)]


def turned(u):
    return 1 if UNITS[u][1] == 0 else 2


BETWEEN = [[f"g{n}"] for n in range(16)] + [["mod1"], ["mt1"], ["mod2"], [], ["mt2"], []]


def plan():
    jobs = ["mod0", "mt0", "p.qi0", "p.qi1", "r.qi0", "p.ki", "r.qi1", "wi", "r.ki", "p.ka", "p.kb", "r.ka",
            "wrow", "L0.0", "L0.1", "L1.0", "L1.1", "Ls", "r.kb", "v0", "v1", "v2", "score"]
    late = CHUNKS[5:]
    for i, c in enumerate(late):
        jobs += [f"p.{c}"] + ([f"r.{late[i - 1]}"] if i else [])
    jobs += ["r.qb3"]
    for i in range(len(UNITS) + 1):
        if i == 0:
            jobs += BETWEEN[0]
        if i < len(UNITS):
            jobs += [f"s{i}.0", f"s{i}.1"]
        if i:
            jobs += BETWEEN[2 * i]
        if i:
            jobs += [f"t{i - 1}.{n}" for n in range(turned(i - 1))]
        jobs += BETWEEN[2 * i + 1]
        if i:
            jobs += [f"o{i - 1}"]
    for m in range(KD):
        jobs += [f"ya{m}", f"yb{m}"]
    jobs += [f"out{m}" for m in range(KD)]
    jobs += ["router", "h0", "logits"] + [f"h{n}" for n in range(1, 6)] + ["rank"]
    jobs += [f"x{k}.{h}" for k in range(KD) for h in range(2)]
    jobs += [f"c{s}" for s in range(len(SB))]
    jobs += [f"y{s}.{h}" for s in range(len(SB)) for h in range(2)]
    jobs += [f"z{m}" for m in range(KD)]
    return jobs


PLAN = plan()
NBANK = 4


SOFT = [5 if u[1] == 2 else 7 for u in UNITS]
EXPS = [2 if u[1] == 2 else 4 for u in UNITS]
NORM = 4 + KD
IX = 68
R_HOT, R_GAP, R_SEL, ROUTE = 21, 22, 35, 59


def soft_end(u):
    return sum(SOFT[:u + 1])


class Banks:

    def __init__(self, full, drained, psum):
        self.full, self.drained, self.psum = full, drained, psum
        self.place = {name: (i % NBANK, i // NBANK) for i, name in enumerate(PLAN)}
        self.per = [len(range(b, len(PLAN), NBANK)) for b in range(NBANK)]

    def ap(self, name):
        return self.psum[self.place[name][0]][:, :]

    def wait_free(self, eng, l, name):
        b, i = self.place[name]
        eng.wait_ge(self.drained[b], l * self.per[b] + (i + 1))

    def wait_full(self, eng, l, name):
        b, i = self.place[name]
        eng.wait_ge(self.full[b], l * self.per[b] + (i + 1))

    def wait_drained(self, eng, l, name):
        b, i = self.place[name]
        eng.wait_ge(self.drained[b], l * self.per[b] + (i + 2))

    def filled(self, ins, name):
        ins.then_inc(self.full[self.place[name][0]], 1)

    def done(self, ins, name):
        ins.then_inc(self.drained[self.place[name][0]], 1)


class Signal:

    def __init__(self, sem, per, ahead=0):
        self.sem, self.per, self.ahead, self.n = sem, per, ahead, 0

    def up(self, ins):
        self.n += 1
        assert self.n <= self.per, (self.sem.name, self.n)
        ins.then_inc(self.sem, 1)

    def wait(self, eng, l, n=None):
        eng.wait_ge(self.sem, l * self.per + ((self.per if n is None else n) + self.ahead))

    def wait_so_far(self, eng, l):
        self.wait(eng, l, self.n)


def bc(ap, shape):
    return ap.to_broadcast(shape)


def decoder_trunk(nc, wstream, small, consts, pages, page_table, x_in, c_in, gfin,
                  y_out, ka_out, kb_out, ki_out, vp_out, vs_out):
    with ExitStack() as ctx:
        def sb(name, shape, dt=F32):
            return ctx.enter_context(nc.sbuf_tensor(name, shape, dt))

        def sem(name):
            return ctx.enter_context(nc.semaphore(name))

        ring = sb("ring", [128, RING, PAIR])
        x = sb("x", [128, KD, T])
        h = sb("h", [128, KD, T])
        mod = sb("mod", [128, NMOD, NCOND])
        gsc = sb("gsc", [128, 2, KD, NCOND])
        sc = sb("sc", [128, KD, 32])
        sm = sb("sm", [128, S_END])
        cs = sb("cs", [128, C_END])
        gf = sb("gf", [128, KD])
        rms = sb("rms", [128, T])
        ka = sb("ka", [128, T])
        kb = sb("kb", [128, T])
        ki = sb("ki", [128, T])
        v = sb("v", [128, 3, 256])
        wi = sb("wi", [128, 3, 4])
        wrow = sb("wrow", [128, 8])
        qpad_i = sb("qpad_i", [128, NB, 32])
        qpad = sb("qpad", [128, NB, 32])
        stat = sb("stat", [128, 4, GQ])
        top = sb("top", [128, 8])
        table = sb("table", [1, 2, N_EXP + 1], I32)
        ptab = sb("ptab", [1, NB * PAGES], I32)
        dest = sb("dest", [128, 12, 3])
        cnt = sb("cnt", [128, 4, N_EXP])
        mraw = sb("mraw", [128, 512])
        yb = sb("yb", [128, 256])
        work = sb("work", [128, 19392])

        def carve(at, *shape):
            n = int(np.prod(shape))
            a = work[:, at:at + n]
            if len(shape) == 2:
                return a.rearrange("p (a b) -> p a b", b=shape[1])
            if len(shape) == 3:
                return a.rearrange("p (a b c) -> p a b c", b=shape[1], c=shape[2])
            return a

        q = {c: carve(i * T, T) for i, c in enumerate(["qi0", "qi1"] + CHUNKS[5:])}
        q.update(ki=ki[:, :], ka=ka[:, :], kb=kb[:, :])
        gate = carve(2880, 16, T)
        yT = carve(7488, 8, T)
        pg = carve(9792, NB, 3, PAST)
        scores = [carve(15936 + i * 1024, 1024) for i in range(2)]
        probsT = carve(17984, 2, 512)
        probsN = carve(19008, 256)
        bias_a = [carve(19264, 128), carve(0, 256), carve(256, T)]
        idx = [carve(7488, 128), carve(7616, 256), carve(7872, T)]
        picked = carve(8160, T)
        lgT = rms[0:36, :]
        ropecos = [carve(8448 + i * T, T) for i in range(2)]
        xsort = carve(0, KD, SLOTP)
        ysort = carve(5120, KD, SLOTP)
        yrow = carve(0, len(SB), D)
        hrow = carve(10240, 3, D)
        xs = carve(10240, KD, BLK)
        sg = carve(10496, 2, BLK)
        hdn = carve(10560, 2, BLK)
        gu = carve(10624, 512)
        gusum = carve(11136, 4, BLK)
        sel = carve(13312, 3, SLOTS)
        selw = carve(15040, 3, SLOTS)
        comb = carve(16768, len(SB), T)
        iota = carve(18208, SLOTS)
        YHI = 5120 + 4 * SLOTP
        rt = [carve(YHI + i * 128, 128) for i in range(10)]
        eq1 = carve(YHI + 1280, SLOTS)

        P = [ctx.enter_context(nc.psum_tensor(f"ps{i}", [128, 512], F32)) for i in range(8)]
        pgu, pgut, py, pyt = P[4:]
        banks = Banks([sem(f"full{b}") for b in range(NBANK)], [sem(f"drained{b}") for b in range(NBANK)], P[:NBANK])

        w_in = [sem(f"w_in{s}") for s in range(RING)]
        w_free = sem("w_free")
        cond_in = sem("cond_in")
        start_in = sem("start_in")
        extra_in = sem("extra_in")
        small_in = sem("small_in")
        pages1_in = sem("pages1_in")
        pages2_in = sem("pages2_in")
        rows_out = sem("rows_out")
        y_stored = sem("y_stored")
        zeroed = sem("zeroed")
        silu_c = sem("silu_c")
        x_staged = sem("x_staged")
        gu_done, gu_kept, gut_done = sem("gu_done"), sem("gu_kept"), sem("gut_done")
        summed, silu_done, hdn_ready = sem("summed"), sem("silu_done"), sem("hdn_ready")
        y_done, y_kept = sem("y_done"), sem("y_kept")
        yt_done, yt_kept = sem("yt_done"), sem("yt_kept")
        final = sem("final")
        final_rt = sem("final_rt")

        mods = Signal(sem("mods"), 2)
        sq = Signal(sem("sq"), 2 * KD, KD)
        ss = Signal(sem("ss"), 2, 1)
        mean = Signal(sem("mean"), 2)
        root = Signal(sem("root"), 2)
        norm = Signal(sem("norm"), 2 * NORM)
        normed = Signal(sem("normed"), 2 * KD)
        cosed = Signal(sem("cosed"), len(CHUNKS), 1)
        roped = Signal(sem("roped"), len(CHUNKS), 1)
        padded = Signal(sem("padded"), 12)
        ix = Signal(sem("ix"), IX)
        soft = Signal(sem("soft"), sum(SOFT))
        exps = Signal(sem("exps"), sum(EXPS))
        merged = Signal(sem("merged"), 8)
        xmix = Signal(sem("xmix"), 8)
        route = Signal(sem("route"), ROUTE)
        rexp = Signal(sem("rexp"), 2)
        iotas = Signal(sem("iotas"), 2)
        xmoe = Signal(sem("xmoe"), 8, 1)
        xtmp = Signal(sem("xtmp"), 2 * 8)

        block = ctx.enter_context(nc.Block())

        def within(at):
            return nc.s_assert_within(at, 0, SLOTS, skip_runtime_bounds_check_because="blocks start inside the expert's slots")

        ident = cs[:, C_ID:C_ID + 128]
        ones = cs[:, C_ONE:C_ONE + 128]
        cos, sin = cs[:, C_COS:C_COS + T], cs[:, C_SIN:C_SIN + T]
        cbias = [cs[:, C_CB0:C_CB0 + 128], cs[:, C_CB1:C_CB1 + 256], cs[:, C_SM:C_SM + T]]

        def hold(eng, count):
            eng.reg_alu(count, count, 0, ALU.max)

        def diag(t, rows0, rows, at=0, width=16):
            base = t[rows0:rows0 + rows, 0, at:at + 1]
            return bass.AP(base.tensor, base.offset, [list(base.ap[0]), [64, NB // 2], [48, 2], [1, width]])

        def unit_keys(u):
            return [128, 256, T][UNITS[u][1]]

        def by_seq(ap, n):
            return ap.rearrange("p k (b t) -> p k b t", t=TS)

        @block.sync
        def _(sp):
            def load(i, s):
                sp.dma_start(ring[:, s, :], wstream[i]).then_inc(w_in[s], 16)

            sp.dma_start(sc[:, :, :], c_in).then_inc(cond_in, 16)
            sp.dma_start(x[:, :, :], x_in).then_inc(start_in, 16)
            sp.dma_start(cs[:, :], consts).then_inc(start_in, 16)
            sp.wait_ge(small_in, 16)
            for s in range(RING):
                load(s, s)
            with sp.Fori(1, DEPTH * ROUNDS) as r:
                for s in range(RING):
                    sp.wait_ge(w_free, (r - 1) * RING + (s + 1))
                    load(r * RING + s, s)

        @block.gpsimd
        def _(g):
            nc.gpsimd.memset(qpad_i[:, :, :], 0.0).then_inc(zeroed, 1)
            nc.gpsimd.memset(qpad[:, :, :], 0.0).then_inc(zeroed, 1)
            nc.gpsimd.memset(yb[:, :], 0.0).then_inc(zeroed, 1)
            g.sem_inc(cosed.sem, 1)
            g.wait_ge(zeroed, 3)

            def step(signal, ins):
                signal.up(ins)
                signal.wait_so_far(g, l)
                hold(g, seen)

            seen = g.alloc_register("pool_blocks")
            g.reg_mov(seen, 0)
            with g.Fori(0, DEPTH) as l:
                g.wait_ge(xmoe.sem, l * xmoe.per + 1)
                g.dma_start(sm[:, :], small[l]).then_inc(small_in, 16)
                g.wait_ge(start_in, 16 * 2)
                g.wait_ge(extra_in, 16 * 2)

                def load_pages(w0, n, s):
                    for b in range(NB):
                        for p in range(PAGES):
                            page = g.value_load(ptab[0:1, b * PAGES + p:b * PAGES + p + 1], min_val=0, max_val=POOL - 1)
                            src = pages[bass.ds(page + l * POOL, 1), :, w0 * 128:(w0 + n) * 128]
                            g.dma_start(pg[:, b, 0:n, p * PAGE:(p + 1) * PAGE],
                                        src.rearrange("o p (n k) -> p (o n) k", n=n)).then_inc(s, 16)

                hold(g, seen)
                load_pages(0, 3, pages1_in)
                for i, c in enumerate(CHUNKS):
                    banks.wait_drained(g, l, f"p.{c}")
                    if i >= 2:
                        roped.wait(g, l, i - 1)
                    else:
                        g.wait_ge(roped.sem, l * roped.per + 1)
                    step(cosed, nc.gpsimd.tensor_tensor(ropecos[i % 2], q[c], cos, ALU.mult))
                    if c == "kb":
                        for n in range(NIDX):
                            k, p0 = n // 2, (n % 2) * HD
                            roped.wait(g, l, 2)
                            hold(g, seen)
                            step(padded, nc.gpsimd.tensor_copy(
                                diag(qpad_i, p0, HD, n * TS, TS),
                                q[f"qi{k}"][p0:p0 + HD, NP:T].rearrange("p (c b t) -> p c b t", b=2, t=TS)))
                for br in "ba":
                    roped.wait(g, l)
                    if br == "a":
                        banks.wait_full(g, l, "s4.1")
                    hold(g, seen)
                    for j in range(GQ):
                        step(padded, nc.gpsimd.tensor_copy(
                            diag(qpad, 0, 128, j * TS, TS),
                            q[f"q{br}{j}"][:, NP:T].rearrange("p (c b t) -> p c b t", b=2, t=TS)))
                banks.wait_full(g, l, "o4")
                hold(g, seen)
                load_pages(3, 2, pages2_in)

                xmix.wait(g, l)
                hold(g, seen)
                step(iotas, nc.gpsimd.iota(iota, [[1, SLOTS]], base=0, channel_multiplier=0,
                                        allow_small_or_imprecise_dtypes=True))
                step(iotas, nc.gpsimd.memset(xsort[:, :, SLOTS:SLOTP], 0.0))

                route.wait(g, l)
                for k in range(KD):
                    for hf in range(2):
                        banks.wait_drained(g, l, f"x{k}.{hf}")
                hold(g, seen)
                with g.Fori(0, N_EXP) as e:
                    first = g.value_load(table[0:1, 0, bass.ds(e, 1)], min_val=0, max_val=SLOTS)
                    nblk = g.value_load(table[0:1, 1, bass.ds(e, 1)], min_val=1, max_val=MAXBLK)
                    with g.Fori(0, nblk) as b:
                        n = g.snap(seen, min_val=0, max_val=200)
                        at = within(first + b * BLK)
                        g.wait_ge(gu_done, n + 1)
                        nc.gpsimd.tensor_copy(xs[:, :, :], xsort[:, :, bass.ds(at, BLK)]).then_inc(x_staged, 1)
                        g.wait_ge(x_staged, n + 1)
                        g.reg_add(seen, seen, 1)

        @block.tensor
        def _(pe):
            mm = nc.tensor.matmul
            for b in range(NBANK):
                pe.sem_inc(banks.drained[b], 1)
            pe.sem_inc(gu_done, 1)
            pe.sem_inc(hdn_ready, 1)
            pe.wait_ge(start_in, 16 * 2)
            seen = pe.alloc_register("pe_blocks")
            pe.reg_mov(seen, 0)
            blocks = pe.alloc_register("pe_expert_blocks")
            blocks_ahead = pe.alloc_register("pe_expert_blocks_ahead")

            def add_square(k):
                return mm(pgu[:, 0:T], ones, h[:, k, :], start=(k == 0), stop=(k == KD - 1))

            for k in range(KD):
                pe.wait_ge(sq.sem, k + 1)
                last = add_square(k)
            last.then_inc(ss.sem, 1)
            pe.wait_ge(silu_c, 1)
            pe.wait_ge(zeroed, 3)
            with pe.Fori(0, DEPTH) as l:
                issued = []

                def weights(pair):
                    pe.wait_ge(w_in[pair % RING], l * (ROUNDS * 16) + (pair // RING + 1) * 16)
                    return ring[:, pair % RING, :]

                def job(name):
                    assert PLAN[len(issued)] == name, (PLAN[len(issued)], name)
                    issued.append(name)
                    banks.wait_free(pe, l, name)
                    return banks.ap(name)

                def dense(out, w, rhs, stride=128, k0=0, n=KD):
                    for k in range(n):
                        last = mm(out, w[:, (k0 + k) * stride:(k0 + k) * stride + 128], rhs(k),
                                  start=(k == 0), stop=(k == n - 1))
                    return last

                used_up = []

                def free_after(name):
                    used_up.append(name)

                def filled(ins, name):
                    banks.filled(ins, name)
                    for before in used_up:
                        if before != name:
                            banks.wait_full(pe, l, before)
                            pe.sem_inc(w_free, 1)
                            used_up.remove(before)

                def squares(m, n0):
                    if m:
                        sq.wait(pe, l, n0 + m)
                        last = add_square(m - 1)
                        if m == KD:
                            ss.up(last)

                def modulation(r):
                    ps = job(f"mod{r}")
                    for k in range(KD):
                        w = weights((P_MOD0, P_MOD1, P_MOD2)[r] + k)
                        for c in range(4):
                            last = mm(ps[32 * c:32 * c + 32, :], sc[:, k, :], w[:, c * 512:(c + 1) * 512],
                                      start=(k == 0), stop=(k == KD - 1), skip_group_check=True)
                        if k < KD - 1:
                            last.then_inc(w_free, 1)
                    filled(last, f"mod{r}")
                    free_after(f"mod{r}")

                def turn_modulation(r):
                    ps = job(f"mt{r}")
                    banks.wait_drained(pe, l, f"mod{r}")
                    for j in range(4):
                        last = nc.tensor.transpose(ps[:, j * 128:(j + 1) * 128], mraw[:, j * 128:(j + 1) * 128], ident)
                    filled(last, f"mt{r}")

                modulation(0)
                turn_modulation(0)

                def project(c, w, t):
                    ps = job(f"p.{c}")
                    for k in range(KD):
                        if c == "qi0":
                            normed.wait(pe, l, k + 1)
                        last = mm(ps[:, 0:T], w[:, t * 1024 + k * 128:t * 1024 + (k + 1) * 128], h[:, k, :],
                                  start=(k == 0), stop=(k == KD - 1))
                    filled(last, f"p.{c}")

                def rotate(c):
                    ps = job(f"r.{c}")
                    banks.wait_drained(pe, l, f"p.{c}")
                    filled(mm(ps[:, 0:T], cs[:, C_ROT:C_ROT + 128], q[c], start=True, stop=True), f"r.{c}")

                def sample_scores(ps, qp, new_keys, part, p0, n):
                    hold(pe, seen)
                    for new in (True, False):
                        for odd in range(2):
                            for c in range(4):
                                b = 2 * c + odd
                                rhs = new_keys[p0:p0 + n, NP:T] if new else pg[p0:p0 + n, b, part, :]
                                last = mm(ps[32 * c:32 * c + 32, PAST:T] if new else ps[32 * c:32 * c + 32, 0:PAST],
                                          qp[p0:p0 + n, b, :], rhs, start=(odd == 0), stop=(odd == 1), skip_group_check=True)
                    return last

                w = weights(P_QI)
                project("qi0", w, 0)
                project("qi1", w, 1)
                rotate("qi0")
                free_after("p.qi1")
                w = weights(P_KW)
                project("ki", w, 0)
                rotate("qi1")
                ps = job("wi")
                for tb in range(3):
                    n = [128, 128, NS][tb]
                    for k in range(KD):
                        last = mm(ps[0:n, tb * 4:tb * 4 + 4], h[:, k, tb * 128:tb * 128 + n],
                                  w[:, 1024 + k * 4:1024 + k * 4 + 4], start=(k == 0), stop=(k == KD - 1))
                filled(last, "wi")
                rotate("ki")
                free_after("wi")
                w = weights(P_KAB)
                project("ka", w, 0)
                project("kb", w, 1)
                rotate("ka")
                free_after("p.kb")

                ps = job("wrow")
                banks.wait_drained(pe, l, "wi")
                filled(mm(ps[:, 0:4], cs[0:NS, C_ROW:C_ROW + 128], wi[0:NS, 2, :], start=True, stop=True), "wrow")
                for tb in range(2):
                    keys = 128 * (tb + 1)
                    for half in range(2):
                        name, p0 = f"L{tb}.{half}", half * HD
                        ps = job(name)
                        if tb == 0 and half == 0:
                            roped.wait(pe, l, 3)
                        for i in range(2):
                            last = mm(ps[:, i * keys:(i + 1) * keys], q[f"qi{i}"][p0:p0 + HD, tb * 128:(tb + 1) * 128],
                                      ki[p0:p0 + HD, 0:keys], start=True, stop=True)
                        filled(last, name)
                ps = job("Ls")
                padded.wait(pe, l, 4)
                pe.wait_ge(pages1_in, (l + 1) * (16 * NB * PAGES))
                last = sample_scores(ps, qpad_i, ki, 2, 0, 128)
                filled(last, "Ls")
                rotate("kb")
                w = weights(P_V)
                for tb in range(3):
                    n = [128, 128, NS][tb]
                    ps = job(f"v{tb}")
                    for k in range(KD):
                        last = mm(ps[0:n, 0:256], h[:, k, tb * 128:tb * 128 + n], w[:, k * 256:(k + 1) * 256],
                                  start=(k == 0), stop=(k == KD - 1))
                    filled(last, f"v{tb}")
                free_after("v2")
                ps = job("score")
                banks.wait_drained(pe, l, "Ls")
                filled(mm(ps[:, 0:T], cs[:, C_SUM:C_SUM + 128], idx[2], start=True, stop=True), "score")
                late = CHUNKS[5:]
                for i, c in enumerate(late):
                    if i % 2 == 0:
                        w = weights(P_QA + i // 2)
                    project(c, w, i % 2)
                    if i:
                        rotate(late[i - 1])
                    if i % 2:
                        free_after(f"p.{c}")
                rotate(late[-1])

                def between(names):
                    for name in names:
                        if name[0] == "g":
                            n = int(name[1:])
                            w = weights(P_GATE + n // 2)
                            ps = job(name)
                            filled(dense(ps[:, 0:T], w[:, (n % 2) * 1024:(n % 2) * 1024 + 1024], lambda k: h[:, k, :]), name)
                            if n % 2:
                                free_after(name)
                        else:
                            {"mod": modulation, "mt": turn_modulation}[name[:-1]](int(name[-1]))

                def score_jobs(u):
                    br, tb, kv = UNITS[u]
                    kt = {"a": ka, "b": kb}[br]
                    if u == 0:
                        roped.wait(pe, l)
                    if tb < 2:
                        keys, p0 = unit_keys(u), kv * HD
                        for pair in range(2):
                            ps = job(f"s{u}.{pair}")
                            for i in range(2):
                                last = mm(ps[:, i * keys:(i + 1) * keys],
                                          q[f"q{br}{2 * pair + i}"][p0:p0 + HD, tb * 128:(tb + 1) * 128],
                                          kt[p0:p0 + HD, 0:keys], start=True, stop=True)
                            filled(last, f"s{u}.{pair}")
                    else:
                        padded.wait(pe, l, 8 if br == "b" else 12)
                        if br == "a":
                            pe.wait_ge(pages2_in, (l + 1) * (16 * NB * PAGES))
                        for kv in range(2):
                            p0 = kv * HD
                            ps = job(f"s{u}.{kv}")
                            filled(sample_scores(ps, qpad, kt, 0, p0, HD), f"s{u}.{kv}")

                def turn_jobs(u):
                    br, tb, kv = UNITS[u]
                    s = scores[u % 2]
                    if tb < 2:
                        s = s[:, 0:GQ * unit_keys(u)].rearrange("p (h k) -> p h k", h=GQ)
                        for n in range(turned(u)):
                            ps = job(f"t{u}.{n}")
                            if n == 0:
                                soft.wait(pe, l, soft_end(u))
                            for i in range(GQ):
                                last = nc.tensor.transpose(ps[:, i * 128:(i + 1) * 128], s[:, i, n * 128:(n + 1) * 128], ident)
                            filled(last, f"t{u}.{n}")
                    else:
                        s = s[:, 0:2 * T].rearrange("p (g k) -> p g k", g=2)
                        ps = job(f"t{u}.0")
                        soft.wait(pe, l, soft_end(u))
                        for p in range(PAGES):
                            for kv in range(2):
                                last = nc.tensor.transpose(ps[:, (p * 2 + kv) * 128:(p * 2 + kv + 1) * 128],
                                                           s[:, kv, p * 128:(p + 1) * 128], ident)
                        filled(last, f"t{u}.0")
                        ps = job(f"t{u}.1")
                        for kv in range(2):
                            last = nc.tensor.transpose(ps[0:NS, kv * 128:(kv + 1) * 128], s[:, kv, PAST:T], ident)
                        filled(last, f"t{u}.1")

                def value_job(u):
                    br, tb, kv = UNITS[u]
                    v0 = 0 if br == "a" else 128
                    ps = job(f"o{u}")
                    for n in range(turned(u)):
                        banks.wait_drained(pe, l, f"t{u}.{n}")
                    if tb < 2:
                        p0 = kv * HD
                        for n in range(tb + 1):
                            last = mm(ps[p0:p0 + HD, :], v[:, n, v0 + p0:v0 + p0 + HD], probsT[:, n, :],
                                      start=(n == 0), stop=(n == tb))
                    else:
                        for kv in range(2):
                            p0 = kv * HD
                            mm(ps[p0:p0 + HD, 0:128], v[0:NS, 2, v0 + p0:v0 + p0 + HD], probsN[0:NS, kv * 128:(kv + 1) * 128],
                               start=True, stop=False, skip_group_check=True)
                            for b in range(NB):
                                for p in range(PAGES):
                                    c0 = (p * 2 + kv) * 128 + b * 16
                                    last = mm(ps[p0:p0 + HD, b * 16:(b + 1) * 16], pg[:, b, 1, p * 128 + p0:p * 128 + p0 + HD],
                                              probsT[:, :, :].rearrange("p a c -> p (a c)")[:, c0:c0 + 16],
                                              start=False, stop=(b == NB - 1 and p == PAGES - 1), skip_group_check=True)
                    filled(last, f"o{u}")

                for i in range(len(UNITS) + 1):
                    if i == 0:
                        between(BETWEEN[0])
                    if i < len(UNITS):
                        score_jobs(i)
                    if i:
                        between(BETWEEN[2 * i])
                    if i:
                        turn_jobs(i - 1)
                    between(BETWEEN[2 * i + 1])
                    if i:
                        value_job(i - 1)

                for m in range(KD):
                    w = weights(P_PROJ + m // 2)[:, (m % 2) * 1024:(m % 2) * 1024 + 1024]
                    for half, c in enumerate("ab"):
                        ps = job(f"y{c}{m}")
                        if m == 0 and half == 0:
                            banks.wait_drained(pe, l, f"o{len(UNITS) - 1}")
                        last = dense(ps[:, 0:T], w, lambda k: yT[:, 4 * half + k, :], k0=4 * half, n=4)
                        filled(last, f"y{c}{m}")
                    if m % 2:
                        free_after(f"yb{m}")
                for m in range(KD):
                    w = weights(P_OUT + m // 2)[:, (m % 2) * 1024:(m % 2) * 1024 + 1024]
                    ps = job(f"out{m}")
                    if m == 0:
                        merged.wait(pe, l)
                    filled(dense(ps[:, 0:T], w, lambda k: gate[:, k, :]), f"out{m}")
                    if m % 2 and m < KD - 1:
                        free_after(f"out{m}")
                    squares(m, 0)
                squares(KD, 0)
                assert not used_up, used_up

                ps = job("router")
                for k in range(KD):
                    normed.wait(pe, l, KD + k + 1)
                    last = mm(ps[0:36, 0:T], sm[:, S_WR + k * 36:S_WR + (k + 1) * 36], h[:, k, :], start=(k == 0), stop=(k == KD - 1))
                filled(last, "router")

                def turn_h(n):
                    ps = job(f"h{n}")
                    tb, k0 = n // 2, 4 * (n % 2)
                    for i in range(4):
                        last = nc.tensor.transpose(ps[0:TB, i * 128:(i + 1) * 128], h[:, k0 + i, tb * TB:(tb + 1) * TB], ident)
                    filled(last, f"h{n}")

                turn_h(0)
                ps = job("logits")
                banks.wait_drained(pe, l, "router")
                hold(pe, seen)
                for tb in range(3):
                    last = nc.tensor.transpose(ps[0:TB, tb * 36:(tb + 1) * 36], lgT[:, tb * TB:(tb + 1) * TB], ident[0:36, 0:36])
                filled(last, "logits")
                for n in range(1, 6):
                    turn_h(n)
                ps = job("rank")
                route.wait(pe, l, R_HOT)
                hot = rt[9][:, 0:96].rearrange("p (t e) -> p t e", t=3)
                for tb in range(3):
                    for t2 in range(tb + 1):
                        wt = C_LOW if t2 == tb else C_ONE
                        mm(ps[0:TB, tb * 32:(tb + 1) * 32], cs[0:TB, wt:wt + TB], hot[0:TB, t2, :], start=(t2 == 0), stop=(t2 == tb))
                for tb in range(3):
                    last = mm(ps[:, 96:128], cs[0:TB, C_ONE:C_ONE + 128], hot[0:TB, tb, :], start=(tb == 0), stop=(tb == 2))
                filled(last, "rank")
                for k in range(KD):
                    for hf in range(2):
                        ps = job(f"x{k}.{hf}")
                        if k == 0 and hf == 0:
                            route.wait(pe, l, R_SEL)
                            banks.wait_drained(pe, l, "h5")
                        for tb in range(3):
                            last = mm(ps[:, 0:T], hrow[0:TB, tb, k * 128:(k + 1) * 128], sel[0:TB, tb, hf * T:(hf + 1) * T],
                                      start=(tb == 0), stop=(tb == 2))
                        filled(last, f"x{k}.{hf}")
                for s, (s0, ns) in enumerate(SB):
                    ps = job(f"c{s}")
                    if s == 0:
                        route.wait(pe, l)
                    hold(pe, seen)
                    for tb in range(3):
                        last = nc.tensor.transpose(ps[0:ns, tb * TB:(tb + 1) * TB], selw[0:TB, tb, s0:s0 + ns], ident[0:TB, 0:TB])
                    filled(last, f"c{s}")
                hold(pe, seen)

                def turn_y(n):
                    pe.wait_ge(y_kept, n + 1)
                    pe.wait_ge(yt_kept, n + l + 1)
                    for i in range(2):
                        last = nc.tensor.transpose(pyt[:, i * 128:(i + 1) * 128], yb[:, i * 128:(i + 1) * 128], ident)
                    last.then_inc(yt_done, 1)

                def down(slot):
                    for f in range(2):
                        for c in range(4):
                            last = mm(py[32 * c:32 * c + 32, 0:256], hdn[:, f, :],
                                      ring[:, slot, f * D + c * 256:f * D + (c + 1) * 256],
                                      start=(f == 0), stop=(f == 1), skip_group_check=True)
                    last.then_inc(y_done, 1)

                def expert_block(first_slot, down_slot, load=None):
                    n = pe.snap(seen, min_val=0, max_val=200)
                    pe.wait_ge(x_staged, n + 1)
                    for k in range(KD):
                        c = k % 4
                        last = mm(pgu[32 * c:32 * c + 32, :], xs[:, k, :], ring[:, first_slot + k // 4, c * 512:(c + 1) * 512],
                                  start=(k < 4), stop=(k >= 4), skip_group_check=True)
                    last.then_inc(gu_done, 1)
                    if load:
                        load()
                    pe.wait_ge(hdn_ready, n + 1)
                    down(down_slot)
                    pe.wait_ge(gu_kept, n + 1)
                    for i in range(4):
                        last = nc.tensor.transpose(pgut[:, i * 128:(i + 1) * 128], gu[:, i * 128:(i + 1) * 128], ident)
                    last.then_inc(gut_done, 1)
                    turn_y(n)
                    pe.reg_add(seen, seen, 1)

                ahead = pe.value_load(table[0:1, 1, 0:1], min_val=1, max_val=MAXBLK)
                pe.reg_mov(blocks_ahead, ahead)
                with pe.Fori(0, N_EXP * 3 // RING) as er:
                    for j in range(RING // 3):
                        for s in range(3 * j, 3 * j + 3):
                            pe.wait_ge(w_in[s], l * (ROUNDS * 16) + er * 16 + (P_EXP // RING + 1) * 16)
                        hold(pe, seen)
                        pe.reg_mov(blocks, blocks_ahead)

                        def load_blocks():
                            pe.reg_mov(blocks_ahead, pe.value_load(table[0:1, 1, bass.ds(er * (RING // 3) + j + 1, 1)],
                                                                   min_val=1, max_val=MAXBLK))

                        expert_block(3 * j, (3 * j - 1) % RING, load_blocks)
                        more = pe.snap(blocks, min_val=1, max_val=MAXBLK)
                        with pe.If(more > 1):
                            with pe.Fori(1, more) as b:
                                expert_block(3 * j, 3 * j + 2)
                        pe.wait_ge(y_done, pe.snap(seen, min_val=1, max_val=200) + l)
                        pe.sem_inc(w_free, 3)
                total = pe.snap(seen, min_val=1, max_val=200)
                pe.wait_ge(hdn_ready, total + 1)
                down(RING - 1)
                pe.wait_ge(y_done, total + l + 1)
                pe.sem_inc(w_free, 1)
                turn_y(total)
                pe.wait_ge(yt_kept, total + l + 2)

                for s, (s0, ns) in enumerate(SB):
                    for hf in range(2):
                        ps = job(f"y{s}.{hf}")
                        hold(pe, seen)
                        for i in range(4):
                            last = nc.tensor.transpose(ps[0:ns, i * 128:(i + 1) * 128], ysort[:, 4 * hf + i, s0:s0 + ns], ident)
                        banks.filled(last, f"y{s}.{hf}")
                for m in range(KD):
                    ps = job(f"z{m}")
                    if m == 0:
                        for hf in range(2):
                            banks.wait_drained(pe, l, f"y{len(SB) - 1}.{hf}")
                    for s, (s0, ns) in enumerate(SB):
                        last = mm(ps[:, 0:T], yrow[0:ns, s, m * 128:(m + 1) * 128], comb[0:ns, s, :],
                                  start=(s == 0), stop=(s == len(SB) - 1))
                    banks.filled(last, f"z{m}")
                    squares(m, KD)
                squares(KD, KD)
                assert len(issued) == len(PLAN)

        @block.scalar
        def _(a):
            act = nc.scalar.activation
            a.dma_start(gf[:, :], gfin).then_inc(extra_in, 16)
            a.dma_start(ptab[:, :], page_table).then_inc(extra_in, 16)
            a.sem_inc(yt_kept, 1)
            a.wait_ge(zeroed, 3)
            a.wait_ge(cond_in, 16)
            act(sc[:, :, :], sc[:, :, :], ACT.Silu).then_inc(silu_c, 1)
            a.wait_ge(start_in, 16 * 2)
            for k in range(KD):
                act(h[:, k, :], x[:, k, :], ACT.Square).then_inc(sq.sem, 1)
            before = a.alloc_register("act_before")
            seen = a.alloc_register("act_blocks")
            a.reg_mov(seen, 0)
            with a.Fori(0, DEPTH) as l:
                def copy_out(name, out, src):
                    banks.wait_full(a, l, name)
                    banks.done(act(out, src, ACT.Copy), name)

                def square_root(which):
                    mean.wait(a, l, which + 1)
                    root.up(act(rms[:, :], rms[:, :], ACT.Sqrt))

                def shifts(which):
                    shift = (SH1, SH2)[which]
                    for k in range(KD):
                        norm.wait(a, l, NORM * which + 4 + k + 1)
                        normed.up(act(h[:, k, 0:NP], h[:, k, 0:NP], ACT.Identity, bias=mod[:, shift + k, 0:1]))

                def between(names):
                    for name in names:
                        if name[0] == "g":
                            banks.wait_full(a, l, name)
                            banks.done(act(gate[:, int(name[1:]), :], banks.ap(name)[:, 0:T], ACT.Sigmoid), name)
                        elif name[:3] == "mod":
                            copy_out(name, mraw[:, :], banks.ap(name))

                square_root(0)
                between(["mod0"])
                shifts(0)

                def raw(c):
                    copy_out(f"p.{c}", q[c], banks.ap(f"p.{c}")[:, 0:T])

                raw("qi0")
                raw("qi1")
                raw("ki")
                ps = banks.ap("wi")
                banks.wait_full(a, l, "wi")
                act(wi[:, 0:2, :], ps[:, 0:8].rearrange("p (t c) -> p t c", c=4), ACT.Copy)
                banks.done(act(wi[0:NS, 2, :], ps[0:NS, 8:12], ACT.Copy), "wi")
                raw("ka")
                raw("kb")
                for tb in range(2):
                    keys = 128 * (tb + 1)
                    relu = scores[tb][:, 0:NIDX * keys].rearrange("p (i h k) -> p h i k", i=2, h=2)
                    for half in range(2):
                        name = f"L{tb}.{half}"
                        banks.wait_full(a, l, name)
                        banks.done(act(relu[:, half, :, :], banks.ap(name)[:, 0:2 * keys].rearrange("p (i k) -> p i k", i=2),
                                       ACT.Relu), name)
                for tb in range(3):
                    n = [128, 128, NS][tb]
                    copy_out(f"v{tb}", v[0:n, tb, :], banks.ap(f"v{tb}")[0:n, 0:256])
                for c in CHUNKS[5:]:
                    raw(c)
                for i in range(len(UNITS) + 1):
                    between(BETWEEN[2 * i])
                    if i:
                        u = i - 1
                        br, tb, kv = UNITS[u]
                        if tb < 2:
                            for n in range(turned(u)):
                                copy_out(f"t{u}.{n}", probsT[:, n, :], banks.ap(f"t{u}.{n}"))
                        else:
                            copy_out(f"t{u}.0", probsT[:, :, :].rearrange("p a c -> p (a c)")[:, 0:512], banks.ap(f"t{u}.0"))
                            copy_out(f"t{u}.1", probsN[0:NS, :], banks.ap(f"t{u}.1")[0:NS, 0:256])
                    if i < len(UNITS):
                        soft.wait(a, l, soft_end(i) - SOFT[i] + 2)
                        keys = unit_keys(i)
                        n = EXPS[i]
                        s = scores[i % 2][:, 0:n * keys].rearrange("p (h k) -> p h k", h=n)
                        for j in range(n):
                            exps.up(act(s[:, j, :], s[:, j, :], ACT.Exp, bias=stat[:, 1, j:j + 1], accum_out=stat[:, 2, j:j + 1]))
                    between(BETWEEN[2 * i + 1])
                    if i:
                        ps = banks.ap(f"o{u}")
                        y0 = 0 if br == "a" else 4
                        if tb < 2:
                            p0 = kv * HD
                            copy_out(f"o{u}", yT[p0:p0 + HD, y0:y0 + 4, tb * 128:(tb + 1) * 128],
                                     ps[p0:p0 + HD, :].rearrange("p (h t) -> p h t", h=4))
                        else:
                            copy_out(f"o{u}", by_seq(yT[:, y0:y0 + 4, NP:T], 4),
                                     ps[:, 0:128].rearrange("p (b h t) -> p h b t", b=NB, h=4))
                    if i == 6:
                        roped.wait(a, l)
                        banks.wait_drained(a, l, "v0")
                        banks.wait_drained(a, l, "v1")
                        banks.wait_drained(a, l, "v2")
                        for out, src in ((ka_out[l], ka[:, :]), (kb_out[l], kb[:, :]), (ki_out[l], ki[0:HD, :]),
                                         (vp_out[l].rearrange("n p c -> p n c"), v[:, 0:2, :]), (vs_out[l], v[0:NS, 2, :])):
                            a.dma_start(out, src).then_inc(rows_out, 16)

                for k in range(KD):
                    xmix.wait(a, l, k + 1)
                    sq.up(act(h[:, k, :], x[:, k, :], ACT.Square))
                square_root(1)
                shifts(1)
                copy_out("router", lgT, banks.ap("router")[0:36, 0:T])
                copy_out("h0", hrow[0:TB, 0, 0:512], banks.ap("h0")[0:TB, :])
                route.wait(a, l, 3)
                ex = rt[2][0:TB, 0:12]
                rexp.up(act(ex, rt[1][0:TB, 0:12], ACT.Exp))
                for n in range(1, 6):
                    copy_out(f"h{n}", hrow[0:TB, n // 2, (n % 2) * 512:(n % 2 + 1) * 512], banks.ap(f"h{n}")[0:TB, :])
                route.wait(a, l, R_GAP)
                rexp.up(act(dest[0:TB, 6, :], dest[0:TB, 5, :], ACT.Exp))
                for k in range(KD):
                    for hf in range(2):
                        copy_out(f"x{k}.{hf}", xsort[:, k, hf * T:(hf + 1) * T], banks.ap(f"x{k}.{hf}")[:, 0:T])
                def keep_y(n):
                    a.wait_ge(yt_done, n + l + 1)
                    a.wait_ge(yt_kept, n + l + 1)
                    at = a.snap(before, min_val=0, max_val=SLOTS)
                    act(ysort[:, :, bass.ds(at, BLK)].rearrange("p (c i) s -> p c i s", i=2),
                        pyt[:, 0:256].rearrange("p (i c s) -> p c i s", i=2, c=4), ACT.Copy).then_inc(yt_kept, 1)

                for s, (s0, ns) in enumerate(SB):
                    copy_out(f"c{s}", comb[0:ns, s, :], banks.ap(f"c{s}")[0:ns, 0:T])

                a.reg_mov(before, SLOTS)
                with a.Fori(0, N_EXP) as e:
                    first = a.value_load(table[0:1, 0, bass.ds(e, 1)], min_val=0, max_val=SLOTS)
                    nblk = a.value_load(table[0:1, 1, bass.ds(e, 1)], min_val=1, max_val=MAXBLK)
                    with a.Fori(0, nblk) as b:
                        n = a.snap(seen, min_val=0, max_val=200)
                        a.wait_ge(gu_done, n + 2)
                        act(gu, pgu[:, :], ACT.Copy).then_inc(gu_kept, 1)
                        keep_y(n)
                        a.wait_ge(summed, n + 1)
                        act(sg, gusum[:, 0:2, :], ACT.Silu).then_inc(silu_done, 1)
                        a.reg_mov(before, within(first + b * BLK))
                        a.reg_add(seen, seen, 1)
                keep_y(a.snap(seen, min_val=1, max_val=200))
                for s, (s0, ns) in enumerate(SB):
                    copy_out(f"y{s}.0", yrow[0:ns, s, 0:512], banks.ap(f"y{s}.0")[0:ns, :])
                for k in range(KD):
                    xmoe.wait(a, l, k + 1)
                    sq.up(act(h[:, k, :], x[:, k, :], ACT.Square))
                a.wait_ge(rows_out, (l + 1) * (16 * 5))

            a.wait_ge(final, 1)
            act(rms[:, :], rms[:, :], ACT.Sqrt).then_inc(final_rt, 1)
            for k in range(0, KD, 4):
                a.wait_ge(final, 2 + k + 4)
                a.dma_start(y_out[:, k:k + 4, :], h[:, k:k + 4, :]).then_inc(y_stored, 16)
            a.wait_ge(y_stored, 16 * 2)
            a.wait_ge(rows_out, DEPTH * 16 * 5)

        @block.vector
        def _(d):
            V = nc.vector
            d.sem_inc(roped.sem, 1)
            d.sem_inc(xmoe.sem, 1)
            d.sem_inc(y_kept, 1)
            d.wait_ge(start_in, 16 * 2)
            d.wait_ge(extra_in, 16 * 2)
            seen = d.alloc_register("dve_blocks")
            d.reg_mov(seen, 0)
            with d.Fori(0, DEPTH) as l:
                def scales(which):
                    ss.wait(d, l, which)
                    mean.up(V.tensor_scalar(rms[:, :], pgu[:, 0:T], 1.0 / D, EPS, ALU.mult, ALU.add))
                    root.wait(d, l, which + 1)
                    norm.up(V.reciprocal(rms[:, :], rms[:, :]))
                    norm.wait_so_far(d, l)
                    norm.up(V.tensor_tensor(h[:, :, NP:T], x[:, :, NP:T], bc(rms[:, NP:T].unsqueeze(1), [128, KD, NS]), ALU.mult))
                    norm.wait_so_far(d, l)

                def vnorm(which, shift):
                    hs = by_seq(h[:, :, NP:T], KD)
                    shape = [128, KD, NB, TS]
                    norm.up(V.tensor_tensor(hs, hs, bc(gsc[:, which, :, 1:NCOND].unsqueeze(3), shape), ALU.mult))
                    norm.wait_so_far(d, l)
                    norm.up(V.tensor_tensor(hs, hs, bc(mod[:, shift:shift + KD, 1:NCOND].unsqueeze(3), shape), ALU.add))
                    for k in range(KD):
                        norm.up(V.scalar_tensor_tensor(h[:, k, 0:NP], x[:, k, 0:NP], gsc[:, which, k, 0:1], rms[:, 0:NP],
                                                       ALU.mult, ALU.mult))

                def add_bias(r):
                    shape = [128, 4, 4, NCOND]
                    banks.wait_full(d, l, f"mt{r}")
                    banks.done(V.tensor_tensor(
                        mod[:, r * 16:(r + 1) * 16, :].rearrange("p (c j) n -> p c j n", c=4),
                        banks.ap(f"mt{r}").rearrange("p (j c n) -> p c j n", j=4, c=4)[:, :, :, 0:NCOND],
                        bc(sm[:, S_BA + r * 16:S_BA + (r + 1) * 16].rearrange("p (c j) -> p c j", c=4).unsqueeze(3), shape),
                        ALU.add), f"mt{r}")
                    banks.wait_drained(d, l, f"mt{r}")

                def gain(which, g0, s0):
                    mods.up(V.scalar_tensor_tensor(gsc[:, which, :, :], mod[:, s0:s0 + KD, :], 1.0,
                                                   bc(sm[:, g0:g0 + KD].unsqueeze(2), [128, KD, NCOND]), ALU.add, ALU.mult))
                    mods.wait_so_far(d, l)

                scales(0)
                d.wait_ge(small_in, (l + 1) * 16)
                add_bias(0)
                gain(0, S_GM, SC1)
                vnorm(0, SH1)

                def rope(c):
                    banks.wait_full(d, l, f"r.{c}")
                    ps = banks.ap(f"r.{c}")[:, 0:T]
                    roped.wait_so_far(d, l)
                    banks.done(V.tensor_tensor(rot, ps, sin, ALU.mult), f"r.{c}")
                    banks.wait_drained(d, l, f"r.{c}")
                    i = roped.n
                    cosed.wait(d, l, i + 1)
                    roped.up(V.tensor_tensor(q[c], ropecos[i % 2], rot, ALU.add))

                def step(ins):
                    ix.up(ins)
                    ix.wait_so_far(d, l)

                def select():
                    for tb in range(3):
                        keys = [128, 256, T][tb]
                        seen_keys = picked[:, 0:keys]
                        for r in range(KEEP_P // 8):
                            src = seen_keys if r else idx[tb]
                            hold(d, seen)
                            step(V.max(top[:, :], src))
                            hold(d, seen)
                            step(V.match_replace(seen_keys, top[:, :], src, -3.0e38))
                            yield
                        b = bias_a[tb]
                        if tb == 2:
                            hold(d, seen)
                            step(V.max(top[:, :], seen_keys))
                            step(V.scalar_tensor_tensor(b, seen_keys, top[:, 0:1], cs[:, C_REV:C_REV + T], ALU.is_ge, ALU.mult))
                            step(V.tensor_reduce(top[:, 0:1], b, AX, ALU.max))
                            step(V.tensor_scalar(b, b, top[:, 0:1], None, ALU.is_equal))
                            step(V.tensor_tensor(seen_keys, seen_keys, idx[tb], ALU.is_equal))
                            step(V.tensor_tensor(b, seen_keys, b, ALU.subtract))
                        else:
                            step(V.tensor_tensor(b, seen_keys, idx[tb], ALU.is_equal))
                        step(V.scalar_tensor_tensor(b, b, OFF, cbias[tb], ALU.mult, ALU.add))
                        yield

                rot = carve(9024, T)
                for c in ("qi0", "qi1", "ki", "ka"):
                    rope(c)
                ps = banks.ap("wrow")
                banks.wait_full(d, l, "wrow")
                banks.done(V.tensor_tensor(wrow[:, 0:4], ps[:, 0:4], cs[:, C_HEAD:C_HEAD + 4], ALU.mult), "wrow")
                banks.wait_drained(d, l, "wrow")
                step(V.tensor_reduce(wrow[:, 4:5], wrow[:, 0:4], AX, ALU.add))
                banks.wait_drained(d, l, "wi")
                for tb in range(2):
                    keys = 128 * (tb + 1)
                    banks.wait_drained(d, l, f"L{tb}.0")
                    banks.wait_drained(d, l, f"L{tb}.1")
                    for n in range(NIDX):
                        step(V.scalar_tensor_tensor(idx[tb], scores[tb][:, n * keys:(n + 1) * keys], wi[:, tb, n:n + 1],
                                                    idx[tb] if n else cbias[tb], ALU.mult, ALU.add))
                banks.wait_full(d, l, "Ls")
                banks.done(V.tensor_scalar(idx[2], banks.ap("Ls")[:, 0:T], 0.0, wrow[:, 4:5], ALU.max, ALU.mult), "Ls")
                rope("kb")
                banks.wait_full(d, l, "score")
                banks.done(V.tensor_tensor(idx[2], banks.ap("score")[:, 0:T], cbias[2], ALU.add), "score")
                banks.wait_drained(d, l, "score")
                selection = select()
                for c in CHUNKS[5:]:
                    rope(c)
                    for _ in range(3):
                        next(selection, None)
                for _ in selection:
                    pass

                for u, (br, tb, kv) in enumerate(UNITS):
                    keys, n = unit_keys(u), EXPS[u]
                    s = scores[u % 2][:, 0:n * keys].rearrange("p (h k) -> p h k", h=n)
                    bias = (cbias if br == "b" else bias_a)[tb]
                    for i in range(2):
                        w = n // 2
                        banks.wait_full(d, l, f"s{u}.{i}")
                        banks.done(V.scalar_tensor_tensor(
                            s[:, i * w:(i + 1) * w, :], banks.ap(f"s{u}.{i}")[:, 0:w * keys].rearrange("p (h k) -> p h k", h=w),
                            SCALE, bc(bias.unsqueeze(1), [128, w, keys]), ALU.mult, ALU.add), f"s{u}.{i}")
                    banks.wait_drained(d, l, f"s{u}.0")
                    banks.wait_drained(d, l, f"s{u}.1")
                    if u:
                        soft.wait_so_far(d, l)
                    soft.up(V.tensor_reduce(stat[:, 0, 0:n], s, AX, ALU.max))
                    soft.wait_so_far(d, l)
                    soft.up(V.tensor_scalar(stat[:, 1, 0:n], stat[:, 0, 0:n], -1.0, None, ALU.mult))
                    exps.wait(d, l, sum(EXPS[:u + 1]))
                    soft.up(V.reciprocal(stat[:, 3, 0:n], stat[:, 2, 0:n]))
                    soft.wait_so_far(d, l)
                    for j in range(n):
                        soft.up(V.tensor_scalar(s[:, j, :], s[:, j, :], stat[:, 3, j:j + 1], None, ALU.mult))
                    if u == len(UNITS) - 2:
                        add_bias(1)
                add_bias(2)
                gain(1, S_GF, SC2)

                for m in range(KD):
                    for half, c in enumerate("ab"):
                        banks.wait_drained(d, l, f"g{8 * half + m}")
                        banks.wait_full(d, l, f"y{c}{m}")
                        gm = gate[:, 8 * half + m, :]
                        banks.done(V.tensor_tensor(gm, gm, banks.ap(f"y{c}{m}")[:, 0:T], ALU.mult), f"y{c}{m}")
                    banks.wait_drained(d, l, f"ya{m}")
                    banks.wait_drained(d, l, f"yb{m}")
                    merged.up(V.tensor_tensor(gate[:, m, :], gate[:, m, :], gate[:, 8 + m, :], ALU.add))

                def add_gated(name, m, gt, signal):
                    ps = banks.ap(name)
                    banks.wait_full(d, l, name)
                    if m:
                        signal.wait_so_far(d, l)
                    xtmp.up(V.tensor_tensor(tmp4, ps[:, NP:T].rearrange("p (b t) -> p b t", t=TS),
                                            bc(mod[:, gt + m, 1:NCOND].unsqueeze(2), [128, NB, TS]), ALU.mult))
                    banks.done(V.scalar_tensor_tensor(x[:, m, 0:NP], ps[:, 0:NP], mod[:, gt + m, 0:1], x[:, m, 0:NP],
                                                      ALU.mult, ALU.add), name)
                    xtmp.wait_so_far(d, l)
                    signal.up(V.tensor_tensor(x[:, m, NP:T], x[:, m, NP:T], rms[:, 0:NS], ALU.add))

                tmp4 = rms[:, 0:NS].rearrange("p (b t) -> p b t", t=TS)
                for m in range(KD):
                    add_gated(f"out{m}", m, GT1, xmix)

                xmix.wait_so_far(d, l)
                scales(1)
                vnorm(1, SH2)

                def r(ins):
                    route.up(ins)
                    route.wait_so_far(d, l)

                def trio(i):
                    return dest[0:TB, i, :]

                def spread(ap, n):
                    return bc(ap.unsqueeze(2), [TB, 3, n])

                def first_best(vals, best, out, n, tmp):
                    r(V.tensor_reduce(best, vals, AX, ALU.max))
                    r(V.tensor_tensor(tmp, vals, spread(best, n), ALU.subtract))
                    r(V.scalar_tensor_tensor(out, tmp, 0.0, bc(cs[0:TB, C_REV:C_REV + n].unsqueeze(1), [TB, 3, n]),
                                             ALU.is_ge, ALU.mult))
                    r(V.tensor_reduce(trio(4), out, AX, ALU.max))
                    r(V.tensor_tensor(out, out, spread(trio(4), n), ALU.is_equal))

                lg = rt[0][0:TB, 0:108].rearrange("p (t c) -> p t c", t=3)
                d4, e4, g4 = (rt[i][0:TB, 0:12].rearrange("p (t c) -> p t c", t=3) for i in (1, 2, 3))
                le, d32, hot1, hot2, tmp32, hot = (rt[i][0:TB, 0:96].rearrange("p (t c) -> p t c", t=3) for i in (4, 5, 6, 7, 8, 9))
                banks.wait_full(d, l, "logits")
                banks.done(V.tensor_tensor(lg, banks.ap("logits")[0:TB, 0:108].rearrange("p (t c) -> p t c", t=3),
                                           bc(sm[0:TB, S_BR:S_BR + 36].unsqueeze(1), [TB, 3, 36]), ALU.add), "logits")
                banks.wait_drained(d, l, "logits")
                first_best(lg[:, :, 0:4], trio(0), g4, 4, d4)
                r(V.tensor_scalar(g4, g4, -1.0, -OFF, ALU.add, ALU.mult))
                le4 = rt[4][0:TB, 0:96].rearrange("p (t g e) -> p t g e", t=3, g=N_GRP)
                for tb in range(3):
                    route.up(V.tensor_tensor(le4[:, tb], lg[:, tb, 4:36].rearrange("p (g e) -> p g e", g=N_GRP),
                                             bc(g4[:, tb, :].unsqueeze(2), [TB, N_GRP, 8]), ALU.add))
                route.wait_so_far(d, l)
                first_best(le, trio(1), hot1, N_EXP, d32)
                r(V.scalar_tensor_tensor(tmp32, hot1, 3.0 * OFF, le, ALU.mult, ALU.add))
                first_best(tmp32, trio(2), hot2, N_EXP, d32)
                r(V.tensor_tensor(hot, hot1, hot2, ALU.add))
                assert route.n == R_HOT, route.n
                r(V.tensor_tensor(trio(5), trio(2), trio(1), ALU.subtract))
                assert route.n == R_GAP, route.n
                banks.wait_full(d, l, "rank")
                ps = banks.ap("rank")
                r(V.tensor_copy(cnt[:, 0, :], ps[:, 96:128]))
                r(V.tensor_tensor_scan(cnt[:, 1, :], cs[:, C_ONE:C_ONE + N_EXP], cnt[:, 0, :], 0.0, ALU.mult, ALU.add))
                r(V.tensor_tensor(cnt[:, 1, :], cnt[:, 1, :], cnt[:, 0, :], ALU.subtract))
                banks.done(V.tensor_tensor(d32, ps[0:TB, 0:96].rearrange("p (t c) -> p t c", t=3),
                                           bc(cnt[0:TB, 1, :].unsqueeze(1), [TB, 3, N_EXP]), ALU.add), "rank")
                banks.wait_drained(d, l, "rank")
                for i, oh in ((9, hot1), (10, hot2)):
                    r(V.tensor_tensor(tmp32, oh, d32, ALU.mult))
                    r(V.tensor_reduce(trio(i), tmp32, AX, ALU.add))
                iotas.wait(d, l)
                for tb in range(3):
                    route.up(V.tensor_scalar(sel[0:TB, tb, :], iota[0:TB, :], dest[0:TB, 9, tb:tb + 1], None, ALU.is_equal))
                route.wait_so_far(d, l)
                for tb in range(3):
                    route.up(V.scalar_tensor_tensor(sel[0:TB, tb, :], iota[0:TB, :], dest[0:TB, 10, tb:tb + 1], sel[0:TB, tb, :],
                                                    ALU.is_equal, ALU.add))
                assert route.n == R_SEL, route.n
                r(V.tensor_copy(table[:, 0, 0:N_EXP], cnt[0:1, 1, :]))
                r(V.tensor_scalar(cnt[0:1, 2, :], cnt[0:1, 0, :], BLK + 0.5, 1.0, ALU.is_ge, ALU.add))
                for n in range(2, MAXBLK):
                    r(V.scalar_tensor_tensor(cnt[0:1, 2, :], cnt[0:1, 0, :], n * BLK + 0.5, cnt[0:1, 2, :], ALU.is_ge, ALU.add))
                r(V.tensor_copy(table[:, 1, 0:N_EXP], cnt[0:1, 2, :]))
                r(V.tensor_copy(table[:, 1, N_EXP:N_EXP + 1], cs[0:1, C_ONE:C_ONE + 1]))
                rexp.wait(d, l, 1)
                r(V.tensor_reduce(trio(3), e4, AX, ALU.add))
                rexp.wait(d, l)
                r(V.scalar_tensor_tensor(trio(3), trio(6), 1.0, trio(3), ALU.add, ALU.mult))
                r(V.reciprocal(trio(7), trio(3)))
                r(V.tensor_tensor(trio(8), trio(7), trio(6), ALU.mult))
                for tb in range(3):
                    r(V.tensor_scalar(selw[0:TB, tb, :], iota[0:TB, :], dest[0:TB, 9, tb:tb + 1], dest[0:TB, 7, tb:tb + 1],
                                      ALU.is_equal, ALU.mult))
                    r(V.tensor_scalar(eq1[0:TB, :], iota[0:TB, :], dest[0:TB, 10, tb:tb + 1], dest[0:TB, 8, tb:tb + 1],
                                      ALU.is_equal, ALU.mult))
                    r(V.tensor_tensor(selw[0:TB, tb, :], selw[0:TB, tb, :], eq1[0:TB, :], ALU.add))

                hold(d, seen)
                with d.Fori(0, N_EXP) as e:
                    nblk = d.value_load(table[0:1, 1, bass.ds(e, 1)], min_val=1, max_val=MAXBLK)
                    with d.Fori(0, nblk) as b:
                        n = d.snap(seen, min_val=0, max_val=200)
                        d.wait_ge(gut_done, n + 1)
                        V.tensor_reduce(gusum, pgut[:, :].rearrange("p (i c s) -> p i s c", i=4, c=4), AX, ALU.add).then_inc(summed, 1)
                        d.wait_ge(summed, n + 1)
                        d.wait_ge(silu_done, n + 1)
                        V.tensor_tensor(hdn, sg, gusum[:, 2:4, :], ALU.mult).then_inc(hdn_ready, 1)
                        d.wait_ge(y_done, n + l + 2)
                        V.tensor_copy(yb[:, :], py[:, 0:256]).then_inc(y_kept, 1)
                        d.reg_add(seen, seen, 1)
                for s, (s0, ns) in enumerate(SB):
                    banks.wait_full(d, l, f"y{s}.1")
                    banks.done(V.tensor_copy(yrow[0:ns, s, 512:1024], banks.ap(f"y{s}.1")[0:ns, :]), f"y{s}.1")
                for m in range(KD):
                    add_gated(f"z{m}", m, GT2, xmoe)
                for s in (mods, mean, norm, roped, ix, soft, merged, xmix, route, xmoe, xtmp):
                    assert s.n == s.per, (s.sem.name, s.n, s.per)

            d.wait_ge(ss.sem, DEPTH * ss.per + 1)
            V.tensor_scalar(rms[:, :], pgu[:, 0:T], 1.0 / D, EPS, ALU.mult, ALU.add).then_inc(final, 1)
            d.wait_ge(final_rt, 1)
            V.reciprocal(rms[:, :], rms[:, :]).then_inc(final, 1)
            d.wait_ge(final, 2)
            for k in range(KD):
                V.scalar_tensor_tensor(h[:, k, :], x[:, k, :], gf[:, k:k + 1], rms[:, :], ALU.mult, ALU.mult).then_inc(final, 1)



def constants():
    c = np.zeros((128, C_END), np.float32)
    p = np.arange(128)
    c[:, C_ID:C_ID + 128] = np.eye(128)
    for i in range(128):
        if i % HD < HD // 2:
            c[i + HD // 2, C_ROT + i] = -1.0
        else:
            c[i - HD // 2, C_ROT + i] = 1.0
    c[:, C_ONE:C_ONE + 128] = 1.0
    c[:, C_LOW:C_LOW + 128] = p[:, None] < p[None, :]
    seq, head, tok = p // 16, (p // 4) % 4, p % 4
    c[:, C_SUM:C_SUM + 128] = (seq[:, None] == seq[None]) & (tok[:, None] == tok[None])
    for r in range(128):
        c[seq[r] * 4 + tok[r], C_ROW + r] = 1.0
        c[r, C_HEAD + head[r]] = 1.0
    pos = np.concatenate([np.arange(NP), PAST + np.tile(np.arange(TS), NB)]).astype(np.float32)
    half = HD // 2
    inv = np.power(np.float32(10000.0), -np.arange(half, dtype=np.float32) / np.float32(half)).astype(np.float32)
    ang = pos[None, :] * inv[p % half][:, None]
    c[:, C_COS:C_COS + T] = np.cos(ang)
    c[:, C_SIN:C_SIN + T] = np.sin(ang)
    c[:, C_CB0:C_CB0 + 128] = np.where(p[None] <= p[:, None], 0.0, OFF)
    c[:, C_CB1:C_CB1 + 256] = np.where(np.arange(256)[None] <= 128 + p[:, None], 0.0, OFF)
    s = np.arange(NS)
    ok = (s[None] // TS == seq[:, None]) & (s[None] % TS <= tok[:, None])
    c[:, C_SM + PAST:C_SM + T] = np.where(ok, 0.0, OFF)
    c[:, C_REV:C_REV + T] = T - np.arange(T)
    return c


def kernel(x_prompt, x_sample, c_prompt, c_sample, cache_k_a, cache_v_a, cache_idx_k, cache_k_b, cache_v_b,
           page_table, w_ada, b_ada, g_mix, w_in, w_proj_a, w_proj_b, w_out, g_ffn, w_router_group,
           b_router_group, w_router_expert, b_router_expert, w_exp_gate, w_exp_up, w_exp_down, g_final):
    import concourse.bacc as bacc
    from concourse.bass_utils import run_bass_kernel_spmd as run

    def arr(a):
        return np.asarray(a)

    def cols(w):
        return w.reshape(-1, 128, w.shape[-1]).transpose(1, 0, 2)

    xt = np.concatenate([arr(x_prompt).reshape(NP, D), arr(x_sample).reshape(NS, D)]).T
    ct = np.concatenate([arr(c_prompt), arr(c_sample), np.zeros((32 - NCOND, D), np.float32)]).T
    x_l, c_l = np.ascontiguousarray(cols(xt)), np.ascontiguousarray(cols(ct))

    ws = np.zeros((DEPTH, PAIRS, 128, PAIR), np.float32)
    win = arr(w_in)
    at = np.cumsum([0, 512, 128, 128, 256, 64, 4, 512, 128, 128, 1024, 1024])
    QA, KA, VA, QI, KI, WI, QB, KB, VB, GA, GB = (slice(at[i], at[i + 1]) for i in range(11))
    heads = [np.concatenate([np.arange(64 * j, 64 * j + 64), np.arange(64 * (j + 4), 64 * (j + 4) + 64)]) for j in range(4)]

    def put(l, pair, t, w):
        w = cols(w)
        ws[l, pair, :, t * 1024:t * 1024 + w.shape[1] * w.shape[2]] = w.reshape(128, -1)

    for l in range(DEPTH):
        for r, pair in enumerate((P_MOD0, P_MOD1, P_MOD2)):
            ws[l, pair:pair + KD] = arr(w_ada)[l].reshape(KD, 128, 3, PAIR)[:, :, r]
        wl = win[l]
        put(l, P_QI, 0, wl[:, QI][:, :128])
        put(l, P_QI, 1, wl[:, QI][:, 128:])
        put(l, P_KW, 0, np.concatenate([wl[:, KI], wl[:, KI]], axis=1))
        put(l, P_KW, 1, wl[:, WI])
        put(l, P_KAB, 0, wl[:, KA])
        put(l, P_KAB, 1, wl[:, KB])
        put(l, P_V, 0, np.concatenate([wl[:, VA], wl[:, VB]], axis=1))
        for j in range(4):
            put(l, P_QA + j // 2, j % 2, wl[:, QA][:, heads[j]])
            put(l, P_QB + j // 2, j % 2, wl[:, QB][:, heads[j]])
        for m in range(8):
            part = slice(m * 128, (m + 1) * 128)
            put(l, P_GATE + m // 2, m % 2, wl[:, GA][:, part])
            put(l, P_GATE + 4 + m // 2, m % 2, wl[:, GB][:, part])
            put(l, P_PROJ + m // 2, m % 2, np.concatenate([arr(w_proj_a)[l][heads[j]][:, part] for j in range(4)]
                                                          + [arr(w_proj_b)[l][heads[j]][:, part] for j in range(4)]))
            put(l, P_OUT + m // 2, m % 2, arr(w_out)[l][:, part])
        for e in range(N_EXP):
            both = np.concatenate([arr(w_exp_gate)[l, e], arr(w_exp_up)[l, e]], axis=1)
            put(l, P_EXP + 3 * e, 0, both[:D // 2])
            put(l, P_EXP + 3 * e + 1, 0, both[D // 2:])
            put(l, P_EXP + 3 * e + 2, 0, arr(w_exp_down)[l, e])
    ws = ws.reshape(DEPTH * PAIRS, 128, PAIR)

    sm = np.zeros((DEPTH, 128, S_END), np.float32)
    for l in range(DEPTH):
        wr = np.concatenate([arr(w_router_group)[l], arr(w_router_expert)[l]], axis=1)
        sm[l, :, S_WR:S_WR + KD * 36] = cols(wr).reshape(128, -1)
        sm[l, :, S_GM:S_GM + KD] = arr(g_mix)[l].reshape(KD, 128).T
        sm[l, :, S_GF:S_GF + KD] = arr(g_ffn)[l].reshape(KD, 128).T
        sm[l, :, S_BA:S_BA + NMOD] = arr(b_ada)[l].reshape(NMOD, 128).T
        sm[l, :, S_BR:S_BR + 4] = arr(b_router_group)[l][None]
        sm[l, :, S_BR + 4:S_BR + 36] = arr(b_router_expert)[l][None]

    def keys_across(a):
        return arr(a).reshape(DEPTH * POOL, PAGE, -1).transpose(0, 2, 1)

    kip = keys_across(cache_idx_k)
    pages = np.ascontiguousarray(np.concatenate(
        [keys_across(cache_k_b), arr(cache_v_b).reshape(DEPTH * POOL, PAGE, 128), np.concatenate([kip, kip], axis=1),
         keys_across(cache_k_a), arr(cache_v_a).reshape(DEPTH * POOL, PAGE, 128)], axis=2))

    ins = {"wstream": ws, "small": sm, "consts": constants(), "pages": pages,
           "page_table": np.ascontiguousarray(arr(page_table).reshape(1, NB * PAGES)), "x_in": x_l, "c_in": c_l,
           "gfin": np.ascontiguousarray(arr(g_final).reshape(KD, 128).T)}
    outs = {"y": (128, KD, T), "ka": (DEPTH, 128, T), "kb": (DEPTH, 128, T), "ki": (DEPTH, HD, T),
            "vp": (DEPTH, 2, 128, 256), "vs": (DEPTH, NS, 256)}
    nc = bacc.Bacc("TRN2", target_bir_lowering=False, num_devices=1, dynamic_dma_scratch_size=4096)
    i = {n: nc.dram_tensor(n, a.shape, mybir.dt.from_np(a.dtype), kind="ExternalInput").ap() for n, a in ins.items()}
    o = {n: nc.dram_tensor("out_" + n, s, F32, kind="ExternalOutput").ap() for n, s in outs.items()}
    decoder_trunk(nc, i["wstream"], i["small"], i["consts"], i["pages"], i["page_table"], i["x_in"], i["c_in"], i["gfin"],
                  o["y"], o["ka"], o["kb"], o["ki"], o["vp"], o["vs"])
    r = run(nc, [ins], core_ids=[0]).results[0]
    g = {n: np.asarray(r["out_" + n]) for n in outs}

    y = g["y"].transpose(2, 1, 0).reshape(T, D)

    def rows(a):
        return a.transpose(0, 2, 1)

    def prompt(a):
        return np.ascontiguousarray(a[:, :NP]).reshape(DEPTH, 1, NP, -1)

    def sample(a):
        return np.ascontiguousarray(a[:, NP:]).reshape(DEPTH, NB, TS, -1)

    vv = np.concatenate([g["vp"].reshape(DEPTH, NP, 256), g["vs"]], axis=1)
    parts = [rows(g["ka"]), vv[..., :128], rows(g["kb"]), vv[..., 128:], rows(g["ki"])]

    def by_head(a, i):
        return a.reshape(a.shape[:3] + (NKV, HD)) if i < 4 else a

    return (np.ascontiguousarray(y[:NP]).reshape(1, NP, D), np.ascontiguousarray(y[NP:]).reshape(NB, TS, D),
            *(by_head(prompt(a), i) for i, a in enumerate(parts)), *(by_head(sample(a), i) for i, a in enumerate(parts)))
```
